# Optimizing a Trainium2 kernel written in Bass

```python
import math
import jax, jax.numpy as jnp
from jax import lax
import numpy as np

D_MODEL = 2048
BATCH = 1
SEQ = 256
DEPTH = 1

CHUNK = 64
MEM_LEN = 256
N_BRANCH = 4
BRANCH_W = D_MODEL // 2
EPS = 1e-6
NEG = -1e30
SSM_GROUP = 16
SSM_GROUPS = BRANCH_W // SSM_GROUP
SSM_STATE = 64
CONV_W = 3
ATT_HD = 64
ATT_QH = BRANCH_W // ATT_HD
ATT_KVH = 4
ATT_GRP = ATT_QH // ATT_KVH
WINDOW = 128
WINDOW_CHUNKS = WINDOW // CHUNK
SPAN = WINDOW_CHUNKS * CHUNK
N_BUCKETS = 32
MAX_DISTANCE = 128
MEM_HEADS = 4
MEM_HD = BRANCH_W // MEM_HEADS
KV_W = ATT_KVH * ATT_HD
IN_SIZES = ([BRANCH_W] * 2
            + [BRANCH_W] * 4
            + [BRANCH_W, KV_W, KV_W, BRANCH_W]
            + [BRANCH_W] * 2)
IN_COLS = sum(IN_SIZES)

kernel_name = 'hybrid_ssm_conv_swa_mem_gated_block'

def rmsnorm(x, g):
    xf = x.astype(jnp.float32)
    y = xf * lax.rsqrt(jnp.mean(xf * xf, axis=-1, keepdims=True) + EPS)
    return (y * g.astype(jnp.float32)).astype(x.dtype)

def _ssm_combine(e1, e2):
    a1r, a1i, b1r, b1i = e1
    a2r, a2i, b2r, b2i = e2
    ar = a1r * a2r - a1i * a2i
    ai = a1r * a2i + a1i * a2r
    A2r = a2r[:, None]
    A2i = a2i[:, None]
    br = A2r * b1r - A2i * b1i + b2r
    bi = A2r * b1i + A2i * b1r + b2i
    return ar, ai, br, bi

def ssm_branch(u, lam_re, lam_im, log_dt, b_re, b_im, c_re, c_im, d_skip, w_glu):
    bsz, L, _ = u.shape
    uf = u.astype(jnp.float32)
    dt = jnp.exp(log_dt.astype(jnp.float32))[:, None]
    lr = lam_re.astype(jnp.float32)
    li = lam_im.astype(jnp.float32)
    mag = jnp.exp(lr * dt)
    ang = li * dt
    ab_r = mag * jnp.cos(ang)
    ab_i = mag * jnp.sin(ang)
    den = lr * lr + li * li
    nr = ab_r - 1.0
    f_r = (nr * lr + ab_i * li) / den
    f_i = (ab_i * lr - nr * li) / den
    br_ = b_re.astype(jnp.float32)
    bi_ = b_im.astype(jnp.float32)
    bb_r = f_r[..., None] * br_ - f_i[..., None] * bi_
    bb_i = f_r[..., None] * bi_ + f_i[..., None] * br_
    ug = uf.reshape(bsz, L, SSM_GROUPS, SSM_GROUP).transpose(1, 0, 2, 3)
    bu_r = jnp.einsum('lbgh,gph->lbgp', ug, bb_r)
    bu_i = jnp.einsum('lbgh,gph->lbgp', ug, bb_i)
    a_r = jnp.broadcast_to(ab_r, (L, SSM_GROUPS, SSM_STATE))
    a_i = jnp.broadcast_to(ab_i, (L, SSM_GROUPS, SSM_STATE))
    _, _, xr, xi = lax.associative_scan(_ssm_combine, (a_r, a_i, bu_r, bu_i), axis=0)
    y = (jnp.einsum('lbgp,ghp->blgh', xr, c_re.astype(jnp.float32))
         - jnp.einsum('lbgp,ghp->blgh', xi, c_im.astype(jnp.float32)))
    y = y.reshape(bsz, L, BRANCH_W) + d_skip.astype(jnp.float32) * uf
    h = jax.nn.gelu(y).astype(u.dtype)
    ga, gb = jnp.split(h @ w_glu, 2, axis=-1)
    return ga * jax.nn.sigmoid(gb)

def conv_branch(h, bg, cg, conv_w):
    v = cg * h
    yc = lax.conv_general_dilated(v, conv_w[:, None, :], window_strides=(1,),
                                  padding=[(CONV_W - 1, 0)],
                                  dimension_numbers=('NWC', 'WIO', 'NWC'),
                                  feature_group_count=BRANCH_W)
    return bg * yc

def _t5_buckets(rel):
    nb = N_BUCKETS // 2
    max_exact = nb // 2
    sign = (rel > 0).astype(np.int32) * nb
    n = np.abs(rel)
    large = max_exact + (np.log(np.maximum(n, 1) / max_exact)
                         / np.log(MAX_DISTANCE / max_exact) * (nb - max_exact)).astype(np.int32)
    large = np.minimum(large, nb - 1)
    return (sign + np.where(n < max_exact, n, large)).astype(np.int32)

def _shift_chunks(t, s):
    if s == 0:
        return t
    return jnp.concatenate([jnp.zeros_like(t[:, :s]), t[:, :-s]], axis=1)

def swa_branch(q, k, v, q_g, k_g, sinks, rel_bias):
    bsz, L, _ = q.shape
    nc = L // CHUNK
    q = rmsnorm(q.reshape(bsz, L, ATT_QH, ATT_HD), q_g)
    k = rmsnorm(k.reshape(bsz, L, ATT_KVH, ATT_HD), k_g)
    v = v.reshape(bsz, L, ATT_KVH, ATT_HD)
    q = q.reshape(bsz, nc, CHUNK, ATT_KVH, ATT_GRP, ATT_HD)
    k = k.reshape(bsz, nc, CHUNK, ATT_KVH, ATT_HD)
    v = v.reshape(bsz, nc, CHUNK, ATT_KVH, ATT_HD)
    shifts = list(range(WINDOW_CHUNKS - 1, -1, -1))
    kw = jnp.concatenate([_shift_chunks(k, s) for s in shifts], axis=2)
    vw = jnp.concatenate([_shift_chunks(v, s) for s in shifts], axis=2)
    logits = jnp.einsum('bcqkgd,bcskd->bckgqs', q, kw,
                        preferred_element_type=jnp.float32) * (ATT_HD ** -0.5)
    qi = np.arange(CHUNK)[:, None]
    kj = np.arange(SPAN)[None, :]
    buckets = _t5_buckets(kj - (WINDOW_CHUNKS - 1) * CHUNK - qi)
    bias = rel_bias.astype(jnp.float32)[buckets]
    bias = bias.transpose(2, 0, 1).reshape(ATT_KVH, ATT_GRP, CHUNK, SPAN)
    logits = logits + bias
    key_shift = WINDOW_CHUNKS - 1 - np.arange(SPAN) // CHUNK
    valid = jnp.arange(nc)[:, None] >= key_shift[None, :]
    logits = jnp.where(valid[None, :, None, None, None, :], logits, NEG)
    sink = jnp.broadcast_to(sinks.astype(jnp.float32).reshape(ATT_KVH, ATT_GRP)[None, None, :, :, None, None],
                            logits.shape[:-1] + (1,))
    probs = jax.nn.softmax(jnp.concatenate([logits, sink], axis=-1), axis=-1)[..., :-1]
    out = jnp.einsum('bckgqs,bcskd->bcqkgd', probs.astype(vw.dtype), vw)
    return out.reshape(bsz, L, BRANCH_W)

def mem_branch(q, memn, w_mem_kv, q_g, k_g):
    bsz, L, _ = q.shape
    m = memn.shape[1]
    km, vm = jnp.split(memn @ w_mem_kv, 2, axis=-1)
    km = rmsnorm(km.reshape(bsz, m, MEM_HEADS, MEM_HD), k_g)
    vm = vm.reshape(bsz, m, MEM_HEADS, MEM_HD)
    q = rmsnorm(q.reshape(bsz, L, MEM_HEADS, MEM_HD), q_g)
    logits = jnp.einsum('blhd,bmhd->bhlm', q, km,
                        preferred_element_type=jnp.float32) * (MEM_HD ** -0.5)
    probs = jax.nn.softmax(logits, axis=-1)
    out = jnp.einsum('bhlm,bmhd->blhd', probs.astype(vm.dtype), vm)
    return out.reshape(bsz, L, BRANCH_W)

def setup_inputs(seed: int = 0) -> dict:
    key = jax.random.key(seed)
    ks = jax.random.split(key, 32)
    f32 = jnp.float32
    nrm = lambda k, shape, scale: jax.random.normal(k, shape, f32) * scale
    x = jax.random.normal(ks[0], (BATCH, SEQ, D_MODEL), f32)
    mem = jax.random.normal(ks[1], (BATCH, MEM_LEN, D_MODEL), f32)
    norm_g = 1.0 + nrm(ks[2], (DEPTH, D_MODEL), 0.02)
    mem_norm_g = 1.0 + nrm(ks[3], (DEPTH, D_MODEL), 0.02)
    w_in = nrm(ks[4], (DEPTH, D_MODEL, IN_COLS), D_MODEL ** -0.5)
    lam_re = -0.5 + nrm(ks[5], (DEPTH, SSM_GROUPS, SSM_STATE), 0.01)
    lam_im = (math.pi * jnp.arange(SSM_STATE, dtype=f32))[None, None, :] + nrm(ks[6], (DEPTH, SSM_GROUPS, SSM_STATE), 0.01)
    log_dt = jax.random.uniform(ks[7], (DEPTH, SSM_GROUPS), f32, math.log(1e-3), math.log(1e-1))
    b_re = nrm(ks[8], (DEPTH, SSM_GROUPS, SSM_STATE, SSM_GROUP), (2 * SSM_GROUP) ** -0.5)
    b_im = nrm(ks[9], (DEPTH, SSM_GROUPS, SSM_STATE, SSM_GROUP), (2 * SSM_GROUP) ** -0.5)
    c_re = nrm(ks[10], (DEPTH, SSM_GROUPS, SSM_GROUP, SSM_STATE), (SSM_STATE) ** -0.5)
    c_im = nrm(ks[11], (DEPTH, SSM_GROUPS, SSM_GROUP, SSM_STATE), (SSM_STATE) ** -0.5)
    d_skip = nrm(ks[12], (DEPTH, BRANCH_W), 1.0)
    w_glu = nrm(ks[13], (DEPTH, BRANCH_W, 2 * BRANCH_W), BRANCH_W ** -0.5)
    conv_w = nrm(ks[14], (DEPTH, CONV_W, BRANCH_W), CONV_W ** -0.5)
    attn_q_g = 1.0 + nrm(ks[15], (DEPTH, ATT_HD), 0.02)
    attn_k_g = 1.0 + nrm(ks[16], (DEPTH, ATT_HD), 0.02)
    sinks = nrm(ks[17], (DEPTH, ATT_QH), 0.5)
    rel_bias = nrm(ks[18], (N_BUCKETS, ATT_QH), 0.5)
    w_mem_kv = nrm(ks[19], (DEPTH, D_MODEL, 2 * BRANCH_W), D_MODEL ** -0.5)
    mem_q_g = 1.0 + nrm(ks[20], (DEPTH, MEM_HD), 0.02)
    mem_k_g = 1.0 + nrm(ks[21], (DEPTH, MEM_HD), 0.02)
    w_branch = nrm(ks[22], (DEPTH, N_BRANCH, BRANCH_W, D_MODEL), BRANCH_W ** -0.5)
    w_merge = nrm(ks[23], (DEPTH, N_BRANCH, D_MODEL, D_MODEL), D_MODEL ** -0.5)
    b_merge = nrm(ks[24], (DEPTH, N_BRANCH, D_MODEL), 0.02)
    w_out = nrm(ks[25], (DEPTH, D_MODEL, D_MODEL), D_MODEL ** -0.5)
    return {'x': x, 'mem': mem, 'norm_g': norm_g, 'mem_norm_g': mem_norm_g, 'w_in': w_in,
            'lam_re': lam_re, 'lam_im': lam_im, 'log_dt': log_dt, 'b_re': b_re, 'b_im': b_im,
            'c_re': c_re, 'c_im': c_im, 'd_skip': d_skip, 'w_glu': w_glu, 'conv_w': conv_w,
            'attn_q_g': attn_q_g, 'attn_k_g': attn_k_g, 'sinks': sinks, 'rel_bias': rel_bias,
            'w_mem_kv': w_mem_kv, 'mem_q_g': mem_q_g, 'mem_k_g': mem_k_g, 'w_branch': w_branch,
            'w_merge': w_merge, 'b_merge': b_merge, 'w_out': w_out}

def reference(x, mem, norm_g, mem_norm_g, w_in, lam_re, lam_im, log_dt, b_re, b_im, c_re, c_im,
              d_skip, w_glu, conv_w, attn_q_g, attn_k_g, sinks, rel_bias, w_mem_kv, mem_q_g,
              mem_k_g, w_branch, w_merge, b_merge, w_out):
    split_at = [int(s) for s in np.cumsum(IN_SIZES)[:-1]]
    for l in range(DEPTH):
        xn = rmsnorm(x, norm_g[l])
        memn = rmsnorm(mem, mem_norm_g[l])
        (s_u, s_z, c_h, c_b, c_c, c_z, a_q, a_k, a_v, a_z, m_q, m_z) = jnp.split(xn @ w_in[l], split_at, axis=-1)
        y_ssm = ssm_branch(s_u, lam_re[l], lam_im[l], log_dt[l], b_re[l], b_im[l], c_re[l], c_im[l],
                           d_skip[l], w_glu[l]) * jax.nn.silu(s_z)
        y_conv = conv_branch(c_h, c_b, c_c, conv_w[l]) * jax.nn.silu(c_z)
        y_att = swa_branch(a_q, a_k, a_v, attn_q_g[l], attn_k_g[l], sinks[l], rel_bias) * jax.nn.silu(a_z)
        y_mem = mem_branch(m_q, memn, w_mem_kv[l], mem_q_g[l], mem_k_g[l]) * jax.nn.silu(m_z)
        merged = jnp.zeros_like(x)
        for bi, yb in enumerate((y_ssm, y_conv, y_att, y_mem)):
            gate = jax.nn.sigmoid(xn @ w_merge[l, bi] + b_merge[l, bi])
            merged = merged + gate * (yb @ w_branch[l, bi])
        x = x + merged @ w_out[l]
    return x


_drawn_inputs = setup_inputs


def setup_inputs(seed=0):
    import zlib

    import numpy as np

    out = dict(_drawn_inputs(seed))
    spreads = {}
    factors = {'norm_g': 4.235,
     'mem_norm_g': 31.389,
     'lam_re': 64.0,
     'lam_im': 53.416,
     'log_dt': 54.96,
     'b_re': 64.0,
     'b_im': 64.0,
     'c_re': 64.0,
     'c_im': 64.0,
     'attn_q_g': 64.0,
     'attn_k_g': 55.884,
     'sinks': 8.0,
     'mem_q_g': 31.844,
     'mem_k_g': 31.678,
     'b_merge': 8.0,
     'd_skip': 2.695,
     'rel_bias': 8.0}
    for name, (base, spread) in spreads.items():
        noise = np.random.default_rng([zlib.crc32(name.encode()), seed]).standard_normal(out[name].shape)
        drawn = base * np.exp(spread * noise) if base else spread * noise
        out[name] = __import__('jax').numpy.asarray(drawn.astype(out[name].dtype))
    for name, factor in factors.items():
        out[name] = (out[name] * factor).astype(out[name].dtype)
    return out
```

```python
from contextlib import ExitStack, contextmanager

import numpy as np

import concourse.bass as bass
from concourse import mybir

F32 = mybir.dt.float32
F32R = mybir.dt.float32r
I32 = mybir.dt.int32
ALU = mybir.AluOpType
ACT = mybir.ActivationFunctionType
AX = mybir.AxisListType

P = 128
D = 2048
L = 256
W = 1024
KT = D // P
WT = W // P
RT = L // P
GC = 256
HK = 4
RING = 4
CHUNK = 64
HEADS = 16
KVH = 4
HD = 64
MHD = 256
GROUPS = 64
STATES = 64
GH = 16
BUCKETS = 32
MAX_DISTANCE = 128
EPS = 1e-6
NEG = -1e30
WINDOW = 3 * CHUNK
LINE = 320
ROUND = 12582912.0
RSQRT_SEED = 1597463007.0
TWO_PI = 6.283185307179586
PI_BELOW = 3.1415925
GELU_C = 0.7978845608028654

COL_U, COL_SZ, COL_C, COL_AQ = 0, W, 2 * W, 6 * W
COL_AKV = COL_AQ + W
COL_AZ = COL_AKV + 2 * KVH * HD
COL_MQ = COL_AZ + W
PC_G, PC_MG, PC_BM, PC_D, PC_CONV = 0, KT, 2 * KT, 6 * KT, 6 * KT + WT


def t5_buckets(rel):
    nb = BUCKETS // 2
    max_exact = nb // 2
    sign = (rel > 0).astype(np.int32) * nb
    n = np.abs(rel)
    large = max_exact + (np.log(np.maximum(n, 1) / max_exact)
                         / np.log(MAX_DISTANCE / max_exact) * (nb - max_exact)).astype(np.int32)
    large = np.minimum(large, nb - 1)
    return (sign + np.where(n < max_exact, n, large)).astype(np.int32)


def constants():
    p = np.arange(P)
    ident = np.eye(P)
    channel_group = p[:, None] // GH == np.arange(8)[None, :]
    state_group = (np.arange(8)[None, None, :] == 2 * np.arange(4)[None, :, None] + p[:, None, None] // STATES)
    time = np.broadcast_to(np.arange(L), (P, L))
    head_ones = p[:, None] // HD == np.arange(2)[None, :]
    ones = np.ones((P, 2))
    block = np.concatenate([ident, channel_group, state_group.reshape(P, 32), time, head_ones, ones], 1)
    rel = np.arange(LINE) - (P - 1) - CHUNK
    onehot = t5_buckets(rel)[None, :] == np.arange(BUCKETS)[:, None]
    return block.astype(np.float32), onehot.astype(np.float32)


STATE_ROWS = ["lr", "li", "dt", "mag", "frac", "den", "sn", "hs", "fr", "fi"]
EXP_STEPS = 22
CONST_COLS = P + 8 + 32 + L + 2 + 2


class Stage:

    def __init__(self, name, turns, kts, half0, group0):
        self.name, self.turns, self.kts = name, turns, kts
        self.half0, self.group0 = half0, group0
        self.halves = sum(kts) // HK
        self.groups = len(kts)
        assert self.halves % RING == 0 and half0 % RING == 0 and self.groups % 2 == 0

    def half(self, turn, slot):
        return turn * self.halves + (self.half0 + slot)

    def pair(self, turn, g):
        return turn * (self.groups // 2) + (self.group0 + g) // 2


def plan():
    merge = [KT, WT, KT, WT]
    out, half, group = [], 0, 0
    for name, turns, kts in [
        ("km", 2, [KT] * 2), ("vm", 2, [KT] * 2), ("u", 2, [KT] * 2), ("mqz", 4, [KT] * 2),
        ("conv", 4, [KT] * 4), ("aq", 2, [KT] * 2), ("akv", 1, [KT] * 2), ("az", 2, [KT] * 2),
        ("merge_conv", 4, merge), ("merge_mem", 4, merge), ("merge_att", 4, merge),
        ("sz", 2, [KT] * 2), ("glu", 4, [WT] * 2), ("merge_ssm", 4, merge), ("out", 4, [KT] * 2),
    ]:
        st = Stage(name, turns, kts, half, group)
        out.append(st)
        half += turns * st.halves
        group += turns * st.groups
    return out, half


class Progress:

    def __init__(self, sem, steps, base=0):
        self.sem, self.steps, self.base = sem, steps, base
        self.per = sum(n for _, n in steps)
        self.k = 0

    def begin(self):
        self.k = 0

    def count(self, name, nth=None):
        c = 0
        for s, n in self.steps:
            if s == name:
                return c + (n if nth is None else nth + 1)
            c += n
        raise KeyError(name)

    def after(self, unit, name, nth=None):
        return self.sem, unit * self.per + (self.base + self.count(name, nth))

    def units(self, n):
        return self.sem, n * self.per + self.base

    def inc(self, ins, name):
        self.k += 1
        assert self.count(name) - dict(self.steps)[name] < self.k <= self.count(name), (name, self.k)
        return ins.then_inc(self.sem, 1)

    def link(self, eng, ins, name, unit):
        self.inc(ins, name)
        eng.wait_ge(self.sem, unit * self.per + (self.base + self.k))

    def end(self):
        assert self.k == self.per, (self.k, self.per)


@contextmanager
def turns_of(eng, n, first=0):
    if n - first == 1:
        yield first
    else:
        with eng.Fori(first, n) as i:
            yield i


def window_slots(head, tail):
    def work(i, slot):
        sub, s = slot // 6, slot % 6
        if sub or not isinstance(i, int):
            tail(i * 2 + (sub - 1), s)
        head(i, i * 2 + sub, s)
    return work


def hybrid_block(nc, x, mem, norm_g, mem_norm_g, w_in, lam_re, lam_im, log_dt, b_re, b_im, c_re, c_im,
                 d_skip, w_glu, conv_w, attn_q_g, attn_k_g, sinks, rel_bias, w_mem_kv, mem_q_g, mem_k_g,
                 w_branch, w_merge, b_merge, w_out, const_block, const_onehot, out):
    STAGES, HALVES = plan()
    stage = {s.name: s for s in STAGES}
    ctx = ExitStack()
    with ctx:
        def sb(name, shape, dt=F32):
            return ctx.enter_context(nc.sbuf_tensor(name, shape, dt))

        def sem(name):
            return ctx.enter_context(nc.semaphore(name))

        x_hi = sb("x_hi", [P, KT, L], F32R)
        x_lo = sb("x_lo", [P, KT, L], F32R)
        raw = sb("raw", [P, RING, HK * GC])
        w_hi = sb("w_hi", [P, RING, HK * GC], F32R)
        w_lo = sb("w_lo", [P, RING, HK * GC], F32R)
        ya_hi = sb("ya_hi", [P, WT, L], F32R)
        ya_lo = sb("ya_lo", [P, WT, L], F32R)
        yb_hi = sb("yb_hi", [P, WT, L], F32R)
        yb_lo = sb("yb_lo", [P, WT, L], F32R)
        KB = 256
        region_at = nc.sbuf_base
        region = sb("region", [P, 32 * KB])
        assert nc.sbuf_base == region_at + 32 * 1024
        m_hi = nc.alloc_sbuf_tensor_at("m_hi", [P, KT, L], F32R, offset=region_at)
        m_lo = nc.alloc_sbuf_tensor_at("m_lo", [P, KT, L], F32R, offset=region_at + 16 * 1024)
        mq = region[:, 0:8 * KB]
        mz = region[:, 8 * KB:16 * KB]
        aq = region[:, 16 * KB:24 * KB]
        az = region[:, 24 * KB:32 * KB]
        arena = sb("arena", [P, 54 * KB])
        merged = arena[:, 0:16 * KB]
        B0 = 16

        def kb(lo, n):
            return arena[:, (B0 + lo) * KB:(B0 + lo + n) * KB]

        u = arena[:, 42 * KB:50 * KB]
        gate = arena[:, 50 * KB:52 * KB]
        val = arena[:, 52 * KB:54 * KB]
        mem_rows = merged.rearrange("p (r n) -> p r n", r=RT)
        x_rows = arena[:, (B0 + 18) * KB:(B0 + 34) * KB].rearrange("p (r n) -> p r n", r=RT)
        kv_rows = kb(0, 16).rearrange("p (r n) -> p r n", r=RT)
        km_t = merged[:, 0:8 * KB]
        cv = az.rearrange("p (g n) -> p g n", g=4)
        cv_th = kb(24, 2)
        ma_sq, ma_e, ma_pt, ma_sz = kb(16, 2), kb(18, 2), kb(20, 2), kb(22, 2)
        ma_q, ma_v = aq[:, 0:2 * KB], aq[:, 2 * KB:4 * KB]
        k_dup = kb(0, 4)
        v_rows = kb(4, 2).rearrange("p (r n) -> p r n", r=RT)
        bias_t = kb(6, 12).rearrange("p (h n) -> p h n", h=HEADS)
        sw_l = kb(18, 3).rearrange("p (w n) -> p w n", w=4)
        sw_e = kb(21, 4).rearrange("p (w n) -> p w n", w=4)
        sw_sq = kb(25, 1)
        sw_q = mq[:, 0:2 * KB].rearrange("p (e n) -> p e n", e=2)
        sw_pt = mq[:, 2 * KB:5 * KB].rearrange("p (e n) -> p e n", e=2)
        sw_sz = mq[:, 5 * KB:6 * KB]
        k_rows = kb(18, 2).rearrange("p (r n) -> p r n", r=RT)
        k_twice = kb(20, 4).rearrange("p (r k t n) -> p r k t n", r=RT, k=KVH, t=2)
        bu = [mq[:, 0:4 * KB], mq[:, 4 * KB:8 * KB]] + [kb(4 * n, 4) for n in range(6)]
        SA, SB, SC, SD, SE, SF, SG, SH = bu
        masked_b, masked_c = az[:, 0:4 * KB], az[:, 4 * KB:8 * KB]
        phase, whole = aq[:, 0:4 * KB], aq[:, 4 * KB:8 * KB]
        ssm_b = mz[:, 0:4 * KB].rearrange("p (c t h) -> p c t h", c=2, t=32)
        ssm_c = mz[:, 4 * KB:8 * KB].rearrange("p (c t n) -> p c t n", c=2, t=WT)
        sz_gate = aq

        const = sb("const", [P, CONST_COLS])
        ident = const[:, 0:P]
        channel_group = const[:, P:P + 8]
        state_group = const[:, P + 8:P + 40].rearrange("p (s j) -> p s j", s=4)
        time = const[:, P + 40:P + 40 + L]
        head_ones = const[:, P + 40 + L:P + 42 + L]
        ones = const[:, P + 42 + L:P + 44 + L]
        prm = sb("prm", [P, P])
        prm_t = sb("prm_t", [P, P])
        gain = sb("gain", [6, P])
        gain_t = sb("gain_t", [P, 8])
        rb = sb("rb", [BUCKETS, HEADS])
        sink_all = sb("sink_all", [P, HEADS])
        stat = sb("stat", [P, 96])
        ssm_t = sb("ssm_t", [P, 4 * 32])
        onehot = gate[0:BUCKETS, 0:LINE]
        line = val[0:HEADS, 0:LINE]
        line_dram = nc.dram_tensor("line_dram", (HEADS, P, LINE), F32, kind="Internal").ap()
        sw_v = sb("sw_v", [P, RT, HD])
        sp_buf = sb("sp_buf", [32, len(STATE_ROWS) * P])

        def spt(name):
            if name in ("k", "p", "t"):
                n = ("k", "p", "t").index(name)
                return gate[0:32, n * P:(n + 1) * P]
            n = STATE_ROWS.index(name)
            return sp_buf[:, n * P:(n + 1) * P]

        acc = ctx.enter_context(nc.psum_tensor("acc", [P, 4, 512], F32))
        side = ctx.enter_context(nc.psum_tensor("side", [P, 4, 512], F32))
        side_flat = side[:, :, :].rearrange("p b n -> p (b n)")

        s_raw = [sem(f"s_raw{n}") for n in range(RING)]
        s_hi = sem("s_hi")
        s_lo = sem("s_lo")
        s_mm = sem("s_mm")
        s_evac = [sem("s_evac0"), sem("s_evac1")]
        s_pass = sem("s_pass")
        s_prm = sem("s_prm")
        s_lam = sem("s_lam")
        s_qpad = sem("s_qpad")
        s_mem_in = sem("s_mem_in")
        s_x_in = sem("s_x_in")
        s_line = sem("s_line")
        s_bias = sem("s_bias")
        s_bc = sem("s_bc")
        s_xres = sem("s_xres")
        s_out = sem("s_out")
        s_neg = sem("s_neg")
        s_sum = sem("s_sum")
        norm_act = Progress(sem("norm_act"), [("ss", 2), ("hi", KT)])
        norm_dve = Progress(sem("norm_dve"), [("rs", 11), ("scale", 2), ("lo", KT)])
        norm_pe = Progress(sem("norm_pe"), [("tr", KT // 2)])
        prm_pe = Progress(sem("prm_pe"), [("tr", 1), ("line", 1)])
        prm_dve = Progress(sem("prm_dve"), [("copy", 4), ("gains", 2), ("line", 1)])
        kp_act = Progress(sem("kp_act"), [("ss", 8)])
        kp_dve = Progress(sem("kp_dve"), [("rs", 11), ("scale", 8), ("kmt", 2)])
        kp_pe = Progress(sem("kp_pe"), [("tr", 1)])
        ak_act = Progress(sem("ak_act"), [("ss", 8)])
        ak_dve = Progress(sem("ak_dve"), [("rs", 11), ("scale", 8), ("kt", 1)])
        ak_pe = Progress(sem("ak_pe"), [("tr", 1)])
        sp_pool = Progress(sem("sp_pool"), [("dt", EXP_STEPS), ("mag", 2 + EXP_STEPS), ("frac", 11), ("den", 3), ("ab", 5), ("f", 8)])
        sp_act = Progress(sem("sp_act"), [("sin", 2), ("copy", 1)])
        sp_dve = Progress(sem("sp_dve"), [("rden", 1)])
        sp_pe = Progress(sem("sp_pe"), [("tr", 1)])
        bb_pool = Progress(sem("bb_pool"), [("prod", 4), ("sum", 2)])
        cv_act = Progress(sem("cv_act"), [("th", 2), ("hi", 1)])
        cv_dve = Progress(sem("cv_dve"), [("v", 1), ("acc", 6), ("y", 1), ("sz", 1), ("yz", 1), ("lo", 1)], base=1)
        ma_pool = Progress(sem("ma_pool"), [("q", 1), ("sq", 1), ("v", 1)])
        ma_pe = Progress(sem("ma_pe"), [("qk", 1), ("tr", 1), ("pv", 1)], base=1)
        ma_dve = Progress(sem("ma_dve"), [("rs", 11), ("sc", 1), ("mx", 1), ("nb", 1), ("rsum", 1), ("p", 2),
                                          ("sz", 1), ("y", 1), ("lo", 1)], base=1)
        ma_act = Progress(sem("ma_act"), [("exp", 2), ("th", 1), ("pt", 1), ("hi", 1)], base=1)
        sw_pool = Progress(sem("sw_pool"), [("q", 2), ("sq", 1), ("v", 1)])
        sw_qk = Progress(sem("sw_qk"), [("qk", 1)], base=1)
        sw_dve = Progress(sem("sw_dve"), [("rs", 11), ("sc", 1), ("l", 4), ("mx", 2), ("nb", 1), ("ds", 1),
                                          ("sum", 1), ("rsum", 1), ("p", 1)])
        sw_act = Progress(sem("sw_act"), [("exp", 4), ("es", 1)])
        st_pe = Progress(sem("st_pe"), [("tr", 1), ("pv", 1)], base=1)
        st_act = Progress(sem("st_act"), [("th", 1), ("pt", 2)])
        st_dve = Progress(sem("st_dve"), [("sz", 1), ("y", 1)], base=1)
        ss_pool = Progress(sem("ss_pool"), [("mask", 4), ("ph", 1), ("z", 2), ("x", 3)], base=1)
        ss_pe = Progress(sem("ss_pe"), [("tr", 1), ("bu", 1), ("y", 1)], base=1)
        ss_act = Progress(sem("ss_act"), [("bt", 2), ("ct", 2), ("sn", 1), ("hs", 1), ("sq", 1)], base=1)
        ss_dve = Progress(sem("ss_dve"), [("ph", 2), ("c", 1), ("pre", 4), ("scan", 8), ("szr", 1), ("czi", 1), ("xi", 1),
                                          ("ys", 1)], base=1)
        at_act = Progress(sem("at_act"), [("hi", 2)])
        at_dve = Progress(sem("at_dve"), [("lo", 2)])
        ge_act = Progress(sem("ge_act"), [("sq", 1), ("th", 1), ("hi", 1)])
        ge_dve = Progress(sem("ge_dve"), [("a", 2), ("h", 1), ("lo", 1)], base=1)
        zz_act = Progress(sem("zz_act"), [("th", 2)])
        zz_dve = Progress(sem("zz_dve"), [("sz", 2)], base=1)
        gl_act = Progress(sem("gl_act"), [("hi", 1)], base=1)
        gl_dve = Progress(sem("gl_dve"), [("w", 1), ("lo", 1)], base=1)
        mg_act = Progress(sem("mg_act"), [("hi", 4)])
        mg_dve = Progress(sem("mg_dve"), [("lo", 4)])

        def gate_on(eng, s, value):
            eng.wait_ge(s, value)
            eng.sem_inc(s_pass, 1)

        g_in = w_in[0]
        g_kv = w_mem_kv[0]

        def weights(st, turn, g):
            if st.name == "km":
                return g_kv, turn * 512 + g * GC
            if st.name == "vm":
                return g_kv, turn * 512 + (W + g * GC)
            if st.name == "u":
                return g_in, turn * 512 + (COL_U + g * GC)
            if st.name == "sz":
                return g_in, turn * 512 + (COL_SZ + g * GC)
            if st.name == "mqz":
                return g_in, turn * 512 + (COL_MQ + g * GC)
            if st.name == "conv":
                return g_in, turn * GC + (COL_C + g * W)
            if st.name == "aq":
                return g_in, turn * 512 + (COL_AQ + g * GC)
            if st.name == "akv":
                return g_in, COL_AKV + g * GC
            if st.name == "az":
                return g_in, turn * 512 + (COL_AZ + g * GC)
            if st.name == "glu":
                return w_glu[0], turn * GC + g * W
            if st.name == "out":
                return w_out[0], turn * 512 + g * GC
            b = ["merge_ssm", "merge_conv", "merge_att", "merge_mem"].index(st.name)
            return (w_merge if g % 2 == 0 else w_branch)[0, b], turn * 512 + (g // 2) * GC

        block = ctx.enter_context(nc.Block())

        @block.sync
        def _(sp):
            sp.dma_start(mem_rows, mem[0].rearrange("(r p) n -> p r n", p=P)).then_inc(s_mem_in, 16)
            for n, st in enumerate(STAGES):
                with turns_of(sp, st.turns) as i:
                    slot = 0
                    for g, kt in enumerate(st.kts):
                        mat, col = weights(st, i, g)
                        for k in range(0, kt, HK):
                            gate_on(sp, s_lo, st.half(i, slot + 1))
                            src = mat[k * P:(k + HK) * P, bass.ds(col, GC)]
                            sp.dma_start(raw[:, slot % RING, :].rearrange("p (k n) -> p k n", k=HK),
                                         src.rearrange("(k p) n -> p k n", p=P)).then_inc(s_raw[slot % RING], 16)
                            slot += 1

        @block.tensor
        def _(pe):
            def half_products(st, i, slot, g, k0, kts, hi, lo, rows):
                r = slot % RING
                pe.wait_ge(s_lo, st.half(i, slot + 1 + RING))
                for n in range(2):
                    if k0 == 0:
                        pe.wait_ge(s_evac[g % 2], st.pair(i, g) * 2 + (n + 1))
                    for k in range(HK):
                        kk = k0 + k
                        o = acc[:, 2 * (g % 2) + n, 0:GC]
                        first, final = kk == 0, kk == kts - 1
                        if rows:
                            a_hi, a_lo = hi[:, kk, n * P:(n + 1) * P], lo[:, kk, n * P:(n + 1) * P]
                            b_hi, b_lo = w_hi[:, r, k * GC:(k + 1) * GC], w_lo[:, r, k * GC:(k + 1) * GC]
                            pe.matmul(o, a_hi, b_hi, start=first, stop=False)
                            pe.matmul(o, a_hi, b_lo, start=False, stop=False)
                            last = pe.matmul(o, a_lo, b_hi, start=False, stop=final)
                        else:
                            c = k * GC + n * P
                            a_hi, a_lo = w_hi[:, r, c:c + P], w_lo[:, r, c:c + P]
                            b_hi, b_lo = hi[:, kk, :], lo[:, kk, :]
                            pe.matmul(o, a_hi, b_hi, start=first, stop=False)
                            pe.matmul(o, a_hi, b_lo, start=False, stop=False)
                            last = pe.matmul(o, a_lo, b_hi, start=False, stop=final)
                    last.then_inc(s_mm, 1)

            def run(st, operands, rows=False, work=None, peel=False):
                def turn(i):
                    slot = 0
                    for g, kts in enumerate(st.kts):
                        hi, lo = operands(g)
                        for k0 in range(0, kts, HK):
                            half_products(st, i, slot, g, k0, kts, hi, lo, rows)
                            if work:
                                work(i, slot)
                            slot += 1

                if peel:
                    turn(0)
                with turns_of(pe, st.turns, int(peel)) as i:
                    turn(i)

            def norm_transposes(unit, rows):
                norm_pe.begin()
                pe.wait_ge(*norm_dve.after(unit, "scale"))
                for b in range(KT // 2):
                    if b >= 4:
                        pe.wait_ge(*norm_dve.after(unit, "lo", 2 * (b - 4) + 1))
                    for kt in (2 * b, 2 * b + 1):
                        for r in range(RT):
                            c = (kt % 8) * L + r * P
                            last = pe.transpose(side_flat[:, c:c + P], rows[:, r, kt * P:(kt + 1) * P], ident)
                    norm_pe.inc(last, "tr")
                norm_pe.end()

            xs = lambda g: (x_hi, x_lo)
            ms = lambda g: (m_hi, m_lo)
            pe.sem_inc(s_mm, 2 * RING)
            for pr in (ma_pe, sw_qk, st_pe, ss_pe):
                pe.sem_inc(pr.sem, pr.base)
            pe.wait_ge(s_prm, 14 * 16)
            pe.transpose(side[:, 0, 0:P], prm[:, :], ident)
            prm_pe.begin()
            prm_pe.inc(pe.transpose(side[:, 0, P:P + 6], gain[:, :], ident[0:6, 0:6]), "tr")
            prm_pe.inc(pe.matmul(side[0:HEADS, 1, 0:LINE], rb[:, :], onehot, start=True, stop=True), "line")
            pe.wait_ge(*prm_dve.after(0, "line"))
            norm_transposes(0, mem_rows)
            pe.wait_ge(*norm_dve.after(0, "lo"))
            run(stage["km"], ms, rows=True)
            norm_transposes(1, x_rows)
            run(stage["vm"], ms, rows=True)
            pe.wait_ge(*kp_dve.after(0, "scale"))
            for f in range(WT):
                for r in range(RT):
                    last = pe.transpose(side_flat[:, f * L + r * P:f * L + (r + 1) * P],
                                        kv_rows[:, r, f * P:(f + 1) * P], ident)
            kp_pe.begin()
            kp_pe.inc(last, "tr")
            pe.wait_ge(*norm_dve.units(2))
            run(stage["u"], xs)
            run(stage["mqz"], xs)
            pe.wait_ge(*sp_pool.units(1))
            pe.wait_ge(*kp_dve.units(1))
            for n, c in enumerate(["mag", "frac", "fr", "fi"]):
                last = pe.transpose(side[:, 0, n * 32:(n + 1) * 32], spt(c), ident[0:32, 0:32])
            sp_pe.begin()
            sp_pe.inc(last, "tr")

            def mem_attention(i, slot):
                if slot == 1:
                    ma_pe.begin()
                    pe.wait_ge(*ma_pool.after(i, "v"))
                    pe.wait_ge(*ma_dve.units(i))
                    pe.wait_ge(*ma_act.units(i))
                    for r in range(RT):
                        for t in range(2):
                            pe.matmul(side[:, 0, r:r + 1], ma_sq[:, t * L + r * P:t * L + (r + 1) * P], ones[:, 0:1],
                                      start=t == 0, stop=t == 1)
                    for r in range(RT):
                        for t in range(2):
                            last = pe.matmul(side[:, 1, r * L:(r + 1) * L], ma_q[:, t * L + r * P:t * L + (r + 1) * P],
                                             km_t[:, bass.ds(i * (2 * L) + t * L, L)], start=t == 0, stop=t == 1)
                    ma_pe.inc(last, "qk")
                elif slot == 9:
                    pe.wait_ge(*ma_dve.after(i, "p"))
                    for k in range(2):
                        for r in range(RT):
                            last = pe.transpose(side[:, 2, k * L + r * P:k * L + (r + 1) * P],
                                                ma_e[:, r * L + k * P:r * L + (k + 1) * P], ident)
                    ma_pe.inc(last, "tr")
                elif slot == 12:
                    pe.wait_ge(*ma_act.after(i, "pt"))
                    for f in range(2):
                        for k in range(2):
                            last = pe.matmul(side[:, 3, f * L:(f + 1) * L],
                                             ma_v[:, k * L + f * P:k * L + (f + 1) * P],
                                             ma_pt[:, k * L:(k + 1) * L], start=k == 0, stop=k == 1)
                    ma_pe.inc(last, "pv")
                    ma_pe.end()

            pe.wait_ge(*sp_act.units(1))
            pe.wait_ge(*kp_dve.units(1))
            run(stage["conv"], xs, work=mem_attention)
            run(stage["aq"], xs)
            run(stage["akv"], xs, rows=True)
            run(stage["az"], xs)
            pe.wait_ge(*ak_dve.after(0, "scale"))
            pe.wait_ge(*ma_dve.units(4))
            for k in range(KVH):
                for r in range(RT):
                    last = pe.transpose(side_flat[:, k * L + r * P:k * L + (r + 1) * P],
                                        k_twice[:, r, k, :, :].rearrange("p t n -> p (t n)"), ident)
            ak_pe.begin()
            ak_pe.inc(last, "tr")

            def window_head(i, t, s):
                if s == 0:
                    sw_qk.begin()
                    pe.wait_ge(*sw_pool.after(t, "sq"))
                    if not (isinstance(t, int) and t == 0):
                        pe.wait_ge(*sw_dve.after(t - 1, "l"))
                    for r in range(RT):
                        pe.matmul(side[:, 1 + r, WINDOW:WINDOW + 2], sw_sq[:, r * P:(r + 1) * P], head_ones,
                                  start=True, stop=True)
                    for r in range(RT):
                        for e in range(2):
                            c = e * 256
                            if r == 0:
                                last = pe.matmul(side[:, 1, c + CHUNK:c + WINDOW], sw_q[:, e, 0:P],
                                                 k_dup[:, bass.ds(i * L, P)], start=True, stop=True)
                            else:
                                last = pe.matmul(side[:, 2, c:c + WINDOW], sw_q[:, e, P:2 * P],
                                                 k_dup[:, bass.ds(i * L + CHUNK, WINDOW)], start=True, stop=True)
                    sw_qk.inc(last, "qk")
                    sw_qk.end()

            def window_tail(t, s):
                if s == 1:
                    st_pe.begin()
                    pe.wait_ge(*sw_dve.after(t, "p"))
                    pe.wait_ge(*st_dve.units(t))
                    for e in range(2):
                        b = 3 if e == 0 else 0
                        pe.transpose(side[:, b, 0:P], sw_e[:, e, P:2 * P], ident)
                        pe.transpose(side[:, b, P:2 * P], sw_e[:, 2 + e, 0:P], ident)
                        last = pe.transpose(side[:, b, 2 * P:3 * P], sw_e[:, 2 + e, P:2 * P], ident)
                    st_pe.inc(last, "tr")
                elif s == 3:
                    pe.wait_ge(*st_act.after(t, "pt"))
                    pe.wait_ge(*sw_pool.after(t, "v"))
                    for e in range(2):
                        rows = slice(e * HD, (e + 1) * HD)
                        pe.matmul(side[rows, 3, 0:P], sw_v[:, 0, :], sw_pt[:, e, 0:P], start=True, stop=True)
                        pe.matmul(side[rows, 3, P:2 * P], sw_v[:, 0, :], sw_pt[:, e, P:2 * P], start=True, stop=False)
                        last = pe.matmul(side[rows, 3, P:2 * P], sw_v[:, 1, :], sw_pt[:, e, 2 * P:3 * P],
                                         start=False, stop=True)
                    st_pe.inc(last, "pv")
                    st_pe.end()

            def merge_operands(hi, lo):
                return lambda g: (x_hi, x_lo) if g % 2 == 0 else (hi, lo)

            pe.wait_ge(*ak_dve.units(1))
            pe.wait_ge(*cv_dve.units(4))
            pe.wait_ge(s_neg, 4)
            run(stage["merge_conv"], merge_operands(ya_hi, ya_lo), work=window_slots(window_head, window_tail),
                peel=True)
            for s in range(6):
                window_tail(7, s)

            def state_space(first):
                def work(i, slot):
                    n = i + first
                    if slot == 0:
                        ss_pe.begin()
                        pe.wait_ge(*ss_pool.after(n, "mask"))
                        pe.wait_ge(*ss_dve.units(n))
                        pe.wait_ge(*ss_act.units(n))
                        for b, (src, c) in enumerate([(masked_b, 0), (masked_b, 512),
                                                          (masked_c, 0), (masked_c, 512)]):
                            for s in range(4):
                                last = pe.transpose(side[:, b, s * P:(s + 1) * P],
                                                    src[:, c + s * P:c + (s + 1) * P], ident)
                        ss_pe.inc(last, "tr")
                    elif slot == 3:
                        pe.wait_ge(*ss_act.after(n, "ct"))
                        for c in range(2):
                            for s in range(4):
                                o = (4 * c + s) * L
                                last = pe.matmul(side_flat[:, o:o + L], SC[:, c * 512 + s * P:c * 512 + (s + 1) * P],
                                                 u[:, bass.ds(n * L, L)], start=True, stop=True)
                        ss_pe.inc(last, "bu")
                    elif slot == 11:
                        pe.wait_ge(*ss_pool.after(n, "x"))
                        pe.wait_ge(*ss_dve.after(n, "xi"))
                        for s in range(4):
                            pe.matmul(side[:, 0, 0:L], SD[:, s * P:(s + 1) * P], SA[:, s * L:(s + 1) * L],
                                      start=s == 0, stop=False)
                        for s in range(4):
                            last = pe.matmul(side[:, 0, 0:L], SD[:, 512 + s * P:512 + (s + 1) * P],
                                             SC[:, s * L:(s + 1) * L], start=False, stop=s == 3)
                        ss_pe.inc(last, "y")
                        ss_pe.end()
                return work

            pe.wait_ge(*ma_dve.units(4))
            pe.wait_ge(*st_dve.units(8))
            run(stage["merge_mem"], merge_operands(yb_hi, yb_lo), work=state_space(0))
            pe.wait_ge(*at_dve.units(1))
            run(stage["merge_att"], merge_operands(ya_hi, ya_lo), work=state_space(4))
            run(stage["sz"], xs)
            pe.wait_ge(*ge_dve.units(2))
            run(stage["glu"], lambda g: (yb_hi, yb_lo))
            pe.wait_ge(*gl_dve.units(4))
            run(stage["merge_ssm"], merge_operands(ya_hi, ya_lo))
            pe.wait_ge(*mg_dve.units(1))
            run(stage["out"], ms, rows=True)

        @block.scalar
        def _(act):
            for pr in (ma_act, ss_act, gl_act):
                act.sem_inc(pr.sem, pr.base)
            act.dma_start(const[:, :], const_block).then_inc(s_prm, 16)
            act.dma_start(prm[PC_G:PC_G + KT, :], norm_g.rearrange("a (t p) -> (a t) p", p=P)).then_inc(s_prm, 16)
            act.dma_start(prm[PC_MG:PC_MG + KT, :], mem_norm_g.rearrange("a (t p) -> (a t) p", p=P)).then_inc(s_prm, 16)
            act.dma_start(prm[PC_BM:PC_BM + 4 * KT, :],
                          b_merge.rearrange("a b (t p) -> (a b t) p", p=P)).then_inc(s_prm, 16)
            act.dma_start(prm[PC_D:PC_D + WT, :], d_skip.rearrange("a (t p) -> (a t) p", p=P)).then_inc(s_prm, 16)
            act.dma_start(prm[PC_CONV:PC_CONV + 3 * WT, :],
                          conv_w.rearrange("a b (t p) -> (a b t) p", p=P)).then_inc(s_prm, 16)
            act.dma_start(rb[:, :], rel_bias).then_inc(s_prm, 16)
            act.dma_start(onehot, const_onehot).then_inc(s_prm, 16)
            for n, g in enumerate([attn_q_g, attn_k_g]):
                for h in range(2):
                    act.dma_start(gain[n:n + 1, h * HD:(h + 1) * HD], g).then_inc(s_prm, 16)
            for n, g in enumerate([mem_q_g, mem_k_g]):
                act.dma_start(gain[2 + 2 * n:4 + 2 * n, :], g.rearrange("a (t p) -> (a t) p", p=P)).then_inc(s_prm, 16)
            act.dma_start(x_rows, x[0].rearrange("(r p) n -> p r n", p=P)).then_inc(s_x_in, 16)
            act.dma_start(spt("lr"),
                          lam_re[0].rearrange("(t a) p -> t (a p)", a=2)).then_inc(s_lam, 16)
            act.dma_start(spt("li"),
                          lam_im[0].rearrange("(t a) p -> t (a p)", a=2)).then_inc(s_lam, 16)
            act.dma_start(spt("dt")[:, 0:2],
                          log_dt[0].rearrange("(t a) -> t a", a=2)).then_inc(s_lam, 16)
            act.dma_start(sink_all[:, :], bass.AP(tensor=sinks.tensor, offset=0, ap=[[0, P], [1, HEADS]])).then_inc(s_lam, 16)

            def split(r, count, free):
                gate_on(act, s_raw[r], count)
                act.wait_ge(s_mm, free)
                act.activation(w_hi[:, r, :], raw[:, r, :], ACT.Copy).then_inc(s_hi, 1)

            def run(st, evac, work=None, ends=False, peel=False):
                def turn(i, last):
                    slot = 0
                    for g, kts in enumerate(st.kts):
                        for k in range(0, kts, HK):
                            if k == kts - HK and evac:
                                for n in range(2):
                                    evac(i, g, n, (s_mm, st.half(i, slot) * 2 + (n + 1 + 2 * RING)))
                            if not (last and slot + RING >= st.halves):
                                q = st.half(i, slot)
                                split(slot % RING, (i * (st.halves // RING) + (st.half0 + slot) // RING + 2) * 16,
                                      q * 2 + (2 + 2 * RING))
                            if work:
                                work(i, slot)
                            slot += 1
                if ends:
                    with turns_of(act, st.turns - 1) as i:
                        turn(i, False)
                    turn(st.turns - 1, True)
                else:
                    if peel:
                        turn(0, False)
                    with turns_of(act, st.turns, int(peel)) as i:
                        turn(i, False)

            def copy_to(dst):
                def evac(i, g, n, done):
                    gate_on(act, *done)
                    act.activation(dst(i, g, n), acc[:, 2 * (g % 2) + n, 0:GC], ACT.Copy).then_inc(s_evac[g % 2], 1)
                return evac

            def norm_sums(unit, rows, arrived):
                norm_act.begin()
                act.wait_ge(arrived, 16)
                act.wait_ge(*(norm_dve.units(1) if unit else prm_dve.units(1)))
                for r in range(RT):
                    norm_act.inc(act.activation(side_flat, rows[:, r, :], ACT.Square,
                                                accum_out=stat[:, 4 * unit + r:4 * unit + r + 1]), "ss")
                    act.wait_ge(*norm_act.after(unit, "ss", r))

            def norm_parts(unit, hi, col):
                for kt in range(KT):
                    act.wait_ge(*norm_pe.after(unit, "tr", kt // 2))
                    c = (kt % 8) * L
                    norm_act.inc(act.activation(hi[:, kt, :], side_flat[:, c:c + L], ACT.Copy,
                                                scale=prm_t[:, col + kt:col + kt + 1]), "hi")
                norm_act.end()

            norm_sums(0, mem_rows, s_mem_in)
            act.dma_start(line_dram, line.rearrange("h (a n) -> h a n", a=1).broadcast_to([HEADS, P, LINE]))\
               .then_inc(s_line, 16)
            for r in range(RING):
                act.wait_ge(s_raw[r], 16)
                act.activation(w_hi[:, r, :], raw[:, r, :], ACT.Copy).then_inc(s_hi, 1)
            norm_parts(0, m_hi, PC_MG)
            run(stage["km"], copy_to(lambda i, g, n: kv_rows[:, n, bass.ds(i * 512 + g * GC, GC)]))
            norm_sums(1, x_rows, s_x_in)
            norm_parts(1, x_hi, PC_G)
            act.wait_ge(s_evac[0], 2 + 4)
            act.wait_ge(s_evac[1], 2 + 4)
            act.wait_ge(*norm_dve.units(2))
            kp_act.begin()
            for r in range(RT):
                for h in range(4):
                    kp_act.inc(act.activation(side[:, 0, 0:MHD], kv_rows[:, r, h * MHD:(h + 1) * MHD], ACT.Square,
                                              accum_out=stat[:, 8 + 4 * r + h:9 + 4 * r + h]), "ss")
                    act.wait_ge(*kp_act.after(0, "ss", 4 * r + h))
            run(stage["vm"], copy_to(lambda i, g, n: kv_rows[:, n, bass.ds(i * 512 + (W + g * GC), GC)]))
            u_v = u.rearrange("p (t n) -> p t n", t=WT)
            run(stage["u"], copy_to(lambda i, g, n: u[:, bass.ds(i * 1024 + (2 * g + n) * L, L)]))
            act.wait_ge(*sp_pool.after(0, "frac"))
            sp_act.begin()
            sp_act.inc(act.activation(spt("sn"), spt("frac"), ACT.Sin, scale=2 * PI_BELOW), "sin")
            sp_act.inc(act.activation(spt("hs"), spt("frac"), ACT.Sin, scale=PI_BELOW), "sin")
            run(stage["mqz"], copy_to(lambda i, g, n: region[:, bass.ds(i * 1024 + (2 * g + n) * L, L)]))
            act.wait_ge(*sp_pe.after(0, "tr"))
            sp_act.inc(act.activation(ssm_t[:, :], side[:, 0, 0:P], ACT.Copy), "copy")

            def conv_evac(i, g, n, done):
                src = acc[:, 2 * (g % 2) + n, 0:GC]
                act.wait_ge(*done)
                if g == 3:
                    if n == 0:
                        cv_act.begin()
                    cv_act.inc(act.activation(cv_th[:, n * L:(n + 1) * L], src, ACT.Tanh, scale=0.5), "th")
                elif n == 0:
                    act.wait_ge(*cv_dve.units(i))
                act.activation(cv[:, g, n * L:(n + 1) * L], src, ACT.Copy).then_inc(s_evac[g % 2], 1)

            def conv_work(i, slot):
                mem_attention(i, slot)
                if slot == 15:
                    gate_on(act, *cv_dve.after(i, "yz"))
                    cv_act.inc(act.activation(ya_hi[:, bass.ds(i * 2, 2), :].rearrange("p t n -> p (t n)"),
                                              cv[:, 2, :], ACT.Copy, scale=0.5), "hi")
                    cv_act.end()

            def mem_attention(i, slot):
                if slot == 5:
                    ma_act.begin()
                    act.wait_ge(*ma_dve.after(i, "nb"))
                    for r in range(RT):
                        ma_act.inc(act.activation(ma_e[:, r * L:(r + 1) * L], side[:, 1, r * L:(r + 1) * L], ACT.Exp,
                                                  scale=stat[:, 34 + r:35 + r], bias=stat[:, 38 + r:39 + r],
                                                  accum_out=stat[:, 40 + r:41 + r]), "exp")
                    act.wait_ge(*ma_act.after(i, "exp"))
                    act.sem_inc(s_pass, 1)
                    ma_act.inc(act.activation(ma_sz, mz[:, bass.ds(i * (2 * L), 2 * L)], ACT.Tanh, scale=0.5), "th")
                elif slot == 10:
                    act.wait_ge(*ma_pe.after(i, "tr"))
                    ma_act.inc(act.activation(ma_pt, side[:, 2, :], ACT.Copy), "pt")
                elif slot == 13:
                    gate_on(act, *ma_dve.after(i, "y"))
                    ma_act.inc(act.activation(yb_hi[:, bass.ds(i * 2, 2), :].rearrange("p t n -> p (t n)"),
                                              ma_sz, ACT.Copy, scale=0.5), "hi")
                    ma_act.end()

            run(stage["conv"], conv_evac, work=conv_work)
            run(stage["aq"], copy_to(lambda i, g, n: aq[:, bass.ds(i * 1024 + (2 * g + n) * L, L)]))

            def akv_evac(i, g, n, done):
                act.wait_ge(*done)
                dst = (k_rows if g == 0 else v_rows)[:, n, :]
                act.activation(dst, acc[:, 2 * (g % 2) + n, 0:GC], ACT.Copy).then_inc(s_evac[g % 2], 1)

            run(stage["akv"], akv_evac)
            act.wait_ge(s_evac[0], 2 * (stage["az"].group0 // 2) + 2)
            ak_act.begin()
            for r in range(RT):
                for h in range(KVH):
                    ak_act.inc(act.activation(side[:, 0, 0:HD], k_rows[:, r, h * HD:(h + 1) * HD], ACT.Square,
                                              accum_out=stat[:, 16 + 4 * r + h:17 + 4 * r + h]), "ss")
                    act.wait_ge(*ak_act.after(0, "ss", 4 * r + h))
            act.wait_ge(s_line, 16)
            act.dma_start(bias_t, bass.AP(tensor=line_dram.tensor, offset=P - 1,
                                          ap=[[LINE - 1, P], [P * LINE, HEADS], [1, WINDOW]])).then_inc(s_bias, 16)
            for c, src in enumerate([b_re, b_im]):
                for a in range(2):
                    act.dma_start(ssm_b[a * STATES:(a + 1) * STATES, c, :, :],
                                  src[0].rearrange("(t a) p h -> a p t h", a=2)[a]).then_inc(s_bc, 16)
            for c, src in enumerate([c_re, c_im]):
                act.dma_start(ssm_c[:, c, :, :],
                              src[0].rearrange("(t g) h p -> (g h) t p", g=8)).then_inc(s_bc, 16)
            run(stage["az"], copy_to(lambda i, g, n: az[:, bass.ds(i * 1024 + (2 * g + n) * L, L)]))

            def gate_evac(name, b):
                def evac(i, g, n, done):
                    if g % 2:
                        return
                    act.wait_ge(*done)
                    gate_on(act, s_evac[1], stage[name].pair(i, g) * 2 + (n + 1))
                    act.activation(gate[:, n * L:(n + 1) * L], acc[:, n, 0:GC], ACT.Tanh, scale=0.5,
                                   bias=prm_t[:, bass.ds(i * 4 + (PC_BM + KT * b + g + n), 1)]).then_inc(s_evac[0], 1)
                return evac

            def window_head(i, t, s):
                if s == 3:
                    sw_act.begin()
                    act.wait_ge(*sw_dve.after(t, "ds"))
                    for w in range(4):
                        sw_act.inc(act.activation(sw_e[:, w, CHUNK:256], sw_l[:, w, :], ACT.Exp,
                                                  bias=stat[:, 60 + w:61 + w], accum_out=stat[:, 64 + w:65 + w]), "exp")
                    sw_act.inc(act.activation(stat[:, 72:76], stat[:, 68:72], ACT.Exp), "es")
                    sw_act.end()

            def window_tail(t, s):
                if s == 0:
                    st_act.begin()
                    gate_on(act, *st_dve.units(t))
                    st_act.inc(act.activation(sw_sz, az[:, bass.ds(t * L, L)], ACT.Tanh, scale=0.5), "th")
                elif s == 2:
                    act.wait_ge(*st_pe.after(t, "tr"))
                    for e in range(2):
                        st_act.inc(act.activation(sw_pt[:, e, :], side[:, 3 if e == 0 else 0, 0:3 * P], ACT.Copy), "pt")
                    st_act.end()

            act.wait_ge(*bb_pool.units(1))
            run(stage["merge_conv"], gate_evac("merge_conv", 1), work=window_slots(window_head, window_tail), peel=True)
            for s in range(6):
                window_tail(7, s)
            at_act.begin()
            act.wait_ge(*st_dve.units(8))
            act.wait_ge(s_mm, 2 * stage["merge_mem"].half0 + 2 * RING)
            for h in range(2):
                at_act.inc(act.activation(ya_hi[:, 4 * h:4 * h + 4, :].rearrange("p t n -> p (t n)"),
                                          aq[:, h * 1024:(h + 1) * 1024], ACT.Copy, scale=0.5), "hi")

            def state_space(first):
                def work(i, slot):
                    n = i + first
                    if slot == 1:
                        ss_act.begin()
                        act.wait_ge(*ss_pe.after(n, "tr"))
                        for c in range(2):
                            ss_act.inc(act.activation(SC[:, c * 512:(c + 1) * 512], side[:, c, :], ACT.Copy), "bt")
                        for c in range(2):
                            ss_act.inc(act.activation(SD[:, c * 512:(c + 1) * 512], side[:, 2 + c, :], ACT.Copy,
                                                      scale=1.0 - 2.0 * c), "ct")
                    elif slot == 2:
                        act.wait_ge(*ss_dve.after(n, "ph"))
                        act.wait_ge(*ss_pool.units(n))
                        ss_act.inc(act.activation(SG, phase, ACT.Sin, scale=2 * PI_BELOW), "sn")
                        ss_act.inc(act.activation(SF, phase, ACT.Sin, scale=PI_BELOW), "hs")
                        act.wait_ge(*ss_act.after(n, "hs"))
                        ss_act.inc(act.activation(SF, SF, ACT.Square), "sq")
                        ss_act.end()
                return work

            run(stage["merge_mem"], gate_evac("merge_mem", 3), work=state_space(0))
            run(stage["merge_att"], gate_evac("merge_att", 2), work=state_space(4))

            def sz_evac(i, g, n, done):
                act.wait_ge(*done)
                if n == 0:
                    gate_on(act, *zz_dve.units(i * 2 + g))
                if n == 0:
                    zz_act.begin()
                zz_act.inc(act.activation(gate[:, n * L:(n + 1) * L], acc[:, 2 * (g % 2) + n, 0:GC], ACT.Tanh, scale=0.5), "th")
                act.sem_inc(s_pass, 1)
                act.activation(sz_gate[:, bass.ds(i * 1024 + (2 * g + n) * L, L)], acc[:, 2 * (g % 2) + n, 0:GC],
                               ACT.Copy).then_inc(s_evac[g % 2], 1)
                if n == 1:
                    zz_act.end()

            def gelu(i, slot):
                ui = u[:, bass.ds(i * 1024, 1024)]
                if slot == 0:
                    ge_act.begin()
                    act.wait_ge(*ss_dve.units(8))
                    gate_on(act, *ge_dve.units(i))
                    ge_act.inc(act.activation(SA, ui, ACT.Square), "sq")
                elif slot == 2:
                    act.wait_ge(*ge_dve.after(i, "a"))
                    ge_act.inc(act.activation(SB, SB, ACT.Tanh, scale=GELU_C), "th")
                elif slot == 5:
                    gate_on(act, *ge_dve.after(i, "h"))
                    ge_act.inc(act.activation(yb_hi[:, bass.ds(i * 4, 4), :].rearrange("p t n -> p (t n)"),
                                              SA, ACT.Copy, scale=0.5), "hi")
                    ge_act.end()

            act.wait_ge(*at_dve.units(1))
            act.wait_ge(s_evac[1], 2 * (stage["sz"].group0 // 2) + 2)
            run(stage["sz"], sz_evac, work=gelu)

            def glu_evac(i, g, n, done):
                if g == 0:
                    return
                act.wait_ge(*done)
                if n == 0:
                    act.wait_ge(*gl_dve.units(i))
                act.activation(gate[:, n * L:(n + 1) * L], acc[:, 2 + n, 0:GC], ACT.Tanh, scale=0.5)\
                   .then_inc(s_evac[1], 1)

            def glu_work(i, slot):
                if slot == 3:
                    gl_act.begin()
                    gate_on(act, *gl_dve.after(i, "w"))
                    gl_act.inc(act.activation(ya_hi[:, bass.ds(i * 2, 2), :].rearrange("p t n -> p (t n)"),
                                              val, ACT.Copy, scale=0.25), "hi")
                    gl_act.end()

            act.wait_ge(*zz_dve.units(4))
            run(stage["glu"], glu_evac, work=glu_work)
            act.wait_ge(*gl_dve.units(4))
            run(stage["merge_ssm"], gate_evac("merge_ssm", 0))
            mg_act.begin()
            for c in range(4):
                act.wait_ge(s_sum, 3 * KT)
                mg_act.inc(act.activation(m_hi[:, 4 * c:4 * c + 4, :].rearrange("p t n -> p (t n)"),
                                          merged[:, c * 1024:(c + 1) * 1024], ACT.Copy, scale=0.5), "hi")
            act.wait_ge(*mg_dve.after(0, "lo"))
            act.dma_start(mem_rows, x[0].rearrange("(r p) n -> p r n", p=P)).then_inc(s_xres, 16)
            run(stage["out"], None, ends=True)

        @block.vector
        def _(dve):
            dve.sem_inc(s_lo, RING)
            dve.sem_inc(s_evac[0], 2)
            dve.sem_inc(s_evac[1], 2)
            for pr in (ma_dve, cv_dve, st_dve, ss_dve, ge_dve, zz_dve, gl_dve):
                dve.sem_inc(pr.sem, pr.base)

            def rest(r):
                return dve.tensor_tensor(w_lo[:, r, :], raw[:, r, :], w_hi[:, r, :].bitcast(F32), ALU.subtract)

            def run(st, evac=None, work=None, ends=False, peel=False):
                def turn(i, last):
                    slot = 0
                    for g, kts in enumerate(st.kts):
                        for k in range(0, kts, HK):
                            if k == kts - HK and evac:
                                for n in range(2):
                                    evac(i, g, n, (s_mm, st.half(i, slot) * 2 + (n + 1 + 2 * RING)))
                            if not (last and slot + RING >= st.halves):
                                dve.wait_ge(s_hi, st.half(i, slot + RING + 1))
                                rest(slot % RING).then_inc(s_lo, 1)
                            if work:
                                work(i, slot)
                            slot += 1
                if ends:
                    with turns_of(dve, st.turns - 1) as i:
                        turn(i, False)
                    turn(st.turns - 1, True)
                else:
                    if peel:
                        turn(0, False)
                    with turns_of(dve, st.turns, int(peel)) as i:
                        turn(i, False)

            def rsqrt(pr, unit, y, a, t, ss, scale):
                pr.link(dve, dve.tensor_scalar(a, ss, scale, EPS, ALU.mult, ALU.add), "rs", unit)
                pr.link(dve, dve.tensor_scalar(y.bitcast(I32), a.bitcast(I32), -0.5, RSQRT_SEED, ALU.mult, ALU.add),
                        "rs", unit)
                for _ in range(3):
                    pr.link(dve, dve.tensor_tensor(t, y, y, ALU.mult), "rs", unit)
                    pr.link(dve, dve.scalar_tensor_tensor(t, t, -0.5, a, ALU.mult, ALU.mult), "rs", unit)
                    pr.link(dve, dve.scalar_tensor_tensor(y, t, 1.5, y, ALU.add, ALU.mult), "rs", unit)

            def norm_scale(unit, rows):
                norm_dve.begin()
                dve.wait_ge(*norm_act.after(unit, "ss"))
                c = 4 * unit
                rsqrt(norm_dve, unit, stat[:, c + 2:c + 4], stat[:, 80:82], stat[:, 82:84], stat[:, c:c + 2], 1.0 / D)
                for r in range(RT):
                    norm_dve.inc(dve.tensor_scalar(rows[:, r, :], rows[:, r, :], stat[:, c + 2 + r:c + 3 + r], None,
                                                   ALU.mult), "scale")

            def norm_parts(unit, hi, lo, col):
                for kt in range(KT):
                    dve.wait_ge(*norm_act.after(unit, "hi", kt | 1))
                    c = (kt % 8) * L
                    norm_dve.inc(dve.scalar_tensor_tensor(lo[:, kt, :], side_flat[:, c:c + L],
                                                          prm_t[:, col + kt:col + kt + 1],
                                                          hi[:, kt, :].bitcast(F32), ALU.mult, ALU.subtract), "lo")
                norm_dve.end()

            prm_dve.begin()
            dve.wait_ge(*prm_pe.after(0, "line"))
            prm_dve.inc(dve.tensor_copy(prm_t[:, 0:PC_BM], side[:, 0, 0:PC_BM]), "copy")
            prm_dve.inc(dve.tensor_scalar(prm_t[:, PC_BM:PC_D], side[:, 0, PC_BM:PC_D], 0.5, None, ALU.mult), "copy")
            prm_dve.inc(dve.tensor_copy(prm_t[:, PC_D:P], side[:, 0, PC_D:P]), "copy")
            prm_dve.link(dve, dve.tensor_copy(gain_t[:, 0:6], side[:, 0, P:P + 6]), "copy", 0)
            prm_dve.inc(dve.tensor_tensor(gain_t[:, 6:7], gain_t[:, 0:1], gain_t[:, 1:2], ALU.mult), "gains")
            prm_dve.inc(dve.tensor_tensor(gain_t[:, 2:4], gain_t[:, 2:4], gain_t[:, 4:6], ALU.mult), "gains")
            prm_dve.inc(dve.tensor_copy(line, side[0:HEADS, 1, 0:LINE]), "line")
            prm_dve.end()
            norm_scale(0, mem_rows)
            for r in range(RING):
                dve.wait_ge(s_hi, r + 1)
                rest(r).then_inc(s_lo, 1)
            norm_parts(0, m_hi, m_lo, PC_MG)
            run(stage["km"])
            norm_scale(1, x_rows)
            norm_parts(1, x_hi, x_lo, PC_G)
            kp_dve.begin()
            dve.wait_ge(*kp_act.after(0, "ss"))
            rsqrt(kp_dve, 0, stat[:, 24:32], stat[:, 80:88], stat[:, 88:96], stat[:, 8:16], 1.0 / MHD)
            for r in range(RT):
                for h in range(4):
                    s = slice(h * MHD, (h + 1) * MHD)
                    kp_dve.inc(dve.tensor_scalar(kv_rows[:, r, s], kv_rows[:, r, s],
                                                 stat[:, 24 + 4 * r + h:25 + 4 * r + h], None, ALU.mult), "scale")
            run(stage["vm"])
            dve.wait_ge(*kp_pe.after(0, "tr"))
            for f in range(2):
                kp_dve.inc(dve.tensor_scalar(
                    km_t.rearrange("p (h f n) -> p h f n", f=2, n=L)[:, :, f, :],
                    side_flat.rearrange("p (h f n) -> p h f n", f=2, n=L)[:, :, f, :],
                    gain_t[:, 2 + f:3 + f], None, ALU.mult), "kmt")
            kp_dve.end()
            run(stage["u"])
            dve.wait_ge(*sp_pool.after(0, "den"))
            sp_dve.begin()
            sp_dve.inc(dve.reciprocal(spt("den"), spt("den")), "rden")
            run(stage["mqz"])

            def conv(i, slot):
                if slot == 12:
                    cv_dve.begin()
                    dve.wait_ge(s_evac[0], stage["conv"].pair(i, 2) * 2 + 4)
                    cv_dve.link(dve, dve.tensor_tensor(cv[:, 0, :], cv[:, 0, :], cv[:, 2, :], ALU.mult), "v", i)
                    for n in range(2):
                        v0, a0 = cv[:, 0, n * L:(n + 1) * L], cv[:, 2, n * L:(n + 1) * L]
                        for k in range(3):
                            w = prm_t[:, bass.ds(i * 2 + (PC_CONV + WT * (2 - k) + n), 1)]
                            if k == 0:
                                ins = dve.tensor_scalar(a0, v0, w, None, ALU.mult)
                            else:
                                ins = dve.scalar_tensor_tensor(a0[:, k:L], v0[:, 0:L - k], w, a0[:, k:L],
                                                               ALU.mult, ALU.add)
                            cv_dve.link(dve, ins, "acc", i)
                elif slot == 13:
                    cv_dve.link(dve, dve.tensor_tensor(cv[:, 2, :], cv[:, 2, :], cv[:, 1, :], ALU.mult), "y", i)
                elif slot == 15:
                    dve.wait_ge(*cv_act.after(i, "th"))
                    dve.wait_ge(s_evac[1], stage["conv"].pair(i, 3) * 2 + 4)
                    cv_dve.link(dve, dve.scalar_tensor_tensor(cv[:, 3, :], cv_th, 1.0, cv[:, 3, :], ALU.add, ALU.mult),
                                "sz", i)
                    cv_dve.inc(dve.tensor_tensor(cv[:, 2, :], cv[:, 2, :], cv[:, 3, :], ALU.mult), "yz")
                    dve.wait_ge(*cv_act.after(i, "hi"))
                    cv_dve.inc(dve.scalar_tensor_tensor(
                        ya_lo[:, bass.ds(i * 2, 2), :].rearrange("p t n -> p (t n)"), cv[:, 2, :], 0.5,
                        ya_hi[:, bass.ds(i * 2, 2), :].rearrange("p t n -> p (t n)").bitcast(F32),
                        ALU.mult, ALU.subtract), "lo")
                    cv_dve.end()

            def mem_attention(i, slot):
                if slot == 3:
                    ma_dve.begin()
                    dve.wait_ge(*ma_pe.after(i, "qk"))
                    rsqrt(ma_dve, i, stat[:, 32:34], stat[:, 80:82], stat[:, 82:84], side[:, 0, 0:2], 1.0 / MHD)
                    ma_dve.inc(dve.tensor_scalar(stat[:, 34:36], stat[:, 32:34], MHD ** -0.5, None, ALU.mult), "sc")
                    ma_dve.link(dve, dve.reduce_max(stat[:, 36:38], side[:, 1, :].rearrange("p (r n) -> p r n", r=RT),
                                                    AX.X), "mx", i)
                    ma_dve.inc(dve.scalar_tensor_tensor(stat[:, 38:40], stat[:, 36:38], -1.0, stat[:, 34:36],
                                                        ALU.mult, ALU.mult), "nb")
                elif slot == 7:
                    dve.wait_ge(*ma_act.after(i, "th"))
                    ma_dve.link(dve, dve.reciprocal(stat[:, 42:44], stat[:, 40:42]), "rsum", i)
                    for r in range(RT):
                        e = ma_e[:, r * L:(r + 1) * L]
                        ma_dve.inc(dve.tensor_scalar(e, e, stat[:, 42 + r:43 + r], None, ALU.mult), "p")
                    ma_dve.inc(dve.scalar_tensor_tensor(ma_sz, ma_sz, 1.0, mz[:, bass.ds(i * (2 * L), 2 * L)],
                                                        ALU.add, ALU.mult), "sz")
                elif slot == 13:
                    dve.wait_ge(*ma_pe.after(i, "pv"))
                    dve.wait_ge(*ma_dve.after(i, "sz"))
                    ma_dve.inc(dve.tensor_tensor(ma_sz, side[:, 3, :], ma_sz, ALU.mult), "y")
                elif slot == 14:
                    dve.wait_ge(*ma_act.after(i, "hi"))
                    ma_dve.inc(dve.scalar_tensor_tensor(
                        yb_lo[:, bass.ds(i * 2, 2), :].rearrange("p t n -> p (t n)"), ma_sz, 0.5,
                        yb_hi[:, bass.ds(i * 2, 2), :].rearrange("p t n -> p (t n)").bitcast(F32),
                        ALU.mult, ALU.subtract), "lo")
                    ma_dve.end()

            def conv_work(i, slot):
                mem_attention(i, slot)
                conv(i, slot)

            run(stage["conv"], work=conv_work)
            run(stage["aq"])
            run(stage["akv"])
            dve.wait_ge(*ak_act.after(0, "ss"))
            ak_dve.begin()
            rsqrt(ak_dve, 0, stat[:, 24:32], stat[:, 80:88], stat[:, 88:96], stat[:, 16:24], 1.0 / HD)
            for r in range(RT):
                for h in range(KVH):
                    ak_dve.inc(dve.tensor_scalar(
                        k_twice[:, r, h, :, :],
                        k_rows[:, r, h * HD:(h + 1) * HD].rearrange("p (a n) -> p a n", a=1).broadcast_to([P, 2, HD]),
                        stat[:, 24 + 4 * r + h:25 + 4 * r + h], None, ALU.mult), "scale")
            run(stage["az"])
            dve.wait_ge(*ak_pe.after(0, "tr"))
            ak_dve.inc(dve.tensor_scalar(k_dup, side_flat[:, 0:KVH * L], gain_t[:, 6:7], None, ALU.mult), "kt")
            ak_dve.end()
            dve.wait_ge(s_bias, 16)
            dve.memset(bias_t[0:CHUNK, :, 2 * CHUNK:WINDOW], NEG).then_inc(s_neg, 1)
            dve.memset(bias_t[CHUNK:P, :, 0:CHUNK], NEG).then_inc(s_neg, 1)
            dve.memset(sw_l[:, 0:2, 0:CHUNK], NEG).then_inc(s_neg, 1)
            dve.memset(sw_e[:, :, 0:CHUNK], 0.0).then_inc(s_neg, 1)
            dve.wait_ge(s_neg, 4)

            def merge_evac(first):
                def evac(i, g, n, done):
                    if g % 2 == 0:
                        return
                    st = stage[first]
                    v = val[:, n * L:(n + 1) * L]
                    m = merged[:, bass.ds(i * 1024 + (g // 2 * 2 + n) * L, L)]
                    dve.wait_ge(*done)
                    dve.wait_ge(s_evac[0], st.pair(i, g - 1) * 2 + (n + 3))
                    if first == "merge_conv":
                        dve.scalar_tensor_tensor(m, gate[:, n * L:(n + 1) * L], 1.0, acc[:, 2 + n, 0:GC],
                                                 ALU.add, ALU.mult).then_inc(s_evac[1], 1)
                        return
                    dve.scalar_tensor_tensor(v, gate[:, n * L:(n + 1) * L], 1.0, acc[:, 2 + n, 0:GC],
                                             ALU.add, ALU.mult).then_inc(s_evac[1], 1)
                    dve.wait_ge(s_evac[1], st.pair(i, g) * 2 + (n + 3))
                    dve.tensor_tensor(m, m, v, ALU.add).then_inc(s_sum, 1)
                return evac

            def window_head(i, t, s):
                sk = sink_all[:, bass.ds(t * 2, 2)].rearrange("p (a n) -> p a n", a=1).broadcast_to([P, 2, 2])
                four = lambda c: stat[:, c:c + 4].rearrange("p (a n) -> p a n", a=2)
                if s == 1:
                    sw_dve.begin()
                    dve.wait_ge(*sw_qk.after(t, "qk"))
                    rsqrt(sw_dve, t, four(44), four(80), four(84), side[:, 1:3, WINDOW:WINDOW + 2], 1.0 / HD)
                    sw_dve.link(dve, dve.tensor_scalar(stat[:, 48:52], stat[:, 44:48], HD ** -0.5, None, ALU.mult),
                                "sc", t)
                    for w in range(4):
                        lo = CHUNK if w < 2 else 0
                        c = (w % 2) * 256
                        sw_dve.inc(dve.scalar_tensor_tensor(
                            sw_l[:, w, lo:WINDOW], side[:, 1 + w // 2, c + lo:c + WINDOW], stat[:, 48 + w:49 + w],
                            bias_t[:, bass.ds(t * 2 + w % 2, 1), lo:WINDOW].rearrange("p a n -> p (a n)"),
                            ALU.mult, ALU.add), "l")
                elif s == 2:
                    dve.wait_ge(*sw_dve.after(t, "l"))
                    sw_dve.link(dve, dve.reduce_max(stat[:, 52:56], sw_l, AX.X), "mx", t)
                    sw_dve.link(dve, dve.tensor_tensor(four(56), four(52), sk, ALU.max), "mx", t)
                    sw_dve.inc(dve.tensor_scalar(stat[:, 60:64], stat[:, 56:60], -1.0, None, ALU.mult), "nb")
                    sw_dve.inc(dve.tensor_tensor(four(68), sk, four(56), ALU.subtract), "ds")
                elif s == 4:
                    dve.wait_ge(*sw_act.after(t, "es"))
                    sw_dve.link(dve, dve.tensor_tensor(stat[:, 64:68], stat[:, 64:68], stat[:, 72:76], ALU.add), "sum", t)
                    sw_dve.link(dve, dve.reciprocal(stat[:, 76:80], stat[:, 64:68]), "rsum", t)
                    rs = stat[:, 76:80].rearrange("p (w a) -> p w a", a=1).broadcast_to([P, 4, WINDOW])
                    sw_dve.inc(dve.tensor_tensor(sw_e[:, :, CHUNK:256], sw_e[:, :, CHUNK:256], rs, ALU.mult), "p")
                    sw_dve.end()

            def window_tail(t, s):
                if s == 1:
                    st_dve.begin()
                    dve.wait_ge(*st_act.after(t, "th"))
                    st_dve.inc(dve.scalar_tensor_tensor(sw_sz, sw_sz, 1.0, az[:, bass.ds(t * L, L)],
                                                        ALU.add, ALU.mult), "sz")
                elif s == 4:
                    dve.wait_ge(*st_pe.after(t, "pv"))
                    dve.wait_ge(*st_dve.after(t, "sz"))
                    st_dve.inc(dve.tensor_tensor(aq[:, bass.ds(t * L, L)], side[:, 3, 0:L], sw_sz, ALU.mult), "y")
                    st_dve.end()

            run(stage["merge_conv"], merge_evac("merge_conv"), work=window_slots(window_head, window_tail), peel=True)
            for s in range(6):
                window_tail(7, s)
            at_dve.begin()
            for h in range(2):
                dve.wait_ge(*at_act.after(0, "hi", h))
                at_dve.inc(dve.scalar_tensor_tensor(
                    ya_lo[:, 4 * h:4 * h + 4, :].rearrange("p t n -> p (t n)"), aq[:, h * 1024:(h + 1) * 1024], 0.5,
                    ya_hi[:, 4 * h:4 * h + 4, :].rearrange("p t n -> p (t n)").bitcast(F32),
                    ALU.mult, ALU.subtract), "lo")
            at_dve.end()

            def state_space(first):
                def work(i, slot):
                    n = i + first
                    if slot == 1:
                        ss_dve.begin()
                        dve.wait_ge(*ss_pool.after(n, "ph"))
                        ss_dve.link(dve, dve.tensor_scalar(whole, phase, ROUND, -ROUND, ALU.add, ALU.add), "ph", n)
                        ss_dve.inc(dve.tensor_tensor(phase, phase, whole, ALU.subtract), "ph")
                    elif slot == 2:
                        dve.wait_ge(*ss_act.after(n, "sq"))
                        ss_dve.link(dve, dve.tensor_scalar(SF, SF, -2.0, 1.0, ALU.mult, ALU.add), "c", n)
                    elif slot == 3:
                        dve.wait_ge(*ss_pe.after(n, "bu"))
                        ss_dve.inc(dve.tensor_tensor(SA, SF, side_flat[:, 0:1024], ALU.mult), "pre")
                        ss_dve.inc(dve.tensor_tensor(SB, SG, side_flat[:, 1024:2048], ALU.mult), "pre")
                    elif slot == 4:
                        ss_dve.inc(dve.tensor_tensor(SE, SF, side_flat[:, 1024:2048], ALU.mult), "pre")
                        ss_dve.inc(dve.tensor_tensor(SH, SG, side_flat[:, 0:1024], ALU.mult), "pre")
                    elif slot in (5, 6):
                        src, dst = (SA, SB) if slot == 5 else (SE, SH)
                        dve.wait_ge(*ss_pool.after(n, "z", slot - 5))
                        for s in range(4):
                            ss_dve.inc(dve.tensor_tensor_scan(
                                dst[:, s * L:(s + 1) * L],
                                ssm_t[:, bass.ds(n * 4 + s, 1)].broadcast_to([P, L]),
                                src[:, s * L:(s + 1) * L], 0.0, ALU.mult, ALU.add), "scan")
                    elif slot == 7:
                        dve.wait_ge(*ss_dve.after(n, "scan"))
                        ss_dve.inc(dve.tensor_tensor(SC, SG, SB, ALU.mult), "szr")
                        ss_dve.link(dve, dve.tensor_tensor(whole, SF, SH, ALU.mult), "czi", n)
                        ss_dve.inc(dve.tensor_tensor(SC, SC, whole, ALU.add), "xi")
                    elif slot == 11:
                        dve.wait_ge(*ss_pe.after(n, "y"))
                        un = u[:, bass.ds(n * L, L)]
                        ss_dve.inc(dve.scalar_tensor_tensor(un, un, prm_t[:, bass.ds(n + PC_D, 1)], side[:, 0, 0:L],
                                                            ALU.mult, ALU.add), "ys")
                        ss_dve.end()
                return work

            run(stage["merge_mem"], merge_evac("merge_mem"), work=state_space(0))
            run(stage["merge_att"], merge_evac("merge_att"), work=state_space(4))

            def sz_evac(i, g, n, done):
                if n == 0:
                    zz_dve.begin()
                dve.wait_ge(s_evac[g % 2], stage["sz"].pair(i, g) * 2 + (n + 3))
                dve.wait_ge(*zz_act.after(i * 2 + g, "th", n))
                z = sz_gate[:, bass.ds(i * 1024 + (2 * g + n) * L, L)]
                zz_dve.inc(dve.scalar_tensor_tensor(z, gate[:, n * L:(n + 1) * L], 1.0, z, ALU.add, ALU.mult), "sz")
                if n == 1:
                    zz_dve.end()

            def gelu(i, slot):
                ui = u[:, bass.ds(i * 1024, 1024)]
                if slot == 1:
                    ge_dve.begin()
                    dve.wait_ge(*ge_act.after(i, "sq"))
                    ge_dve.link(dve, dve.tensor_scalar(SA, SA, 0.044715, 1.0, ALU.mult, ALU.add), "a", i)
                    ge_dve.inc(dve.tensor_tensor(SB, SA, ui, ALU.mult), "a")
                elif slot == 4:
                    dve.wait_ge(*ge_act.after(i, "th"))
                    ge_dve.inc(dve.scalar_tensor_tensor(SA, SB, 1.0, ui, ALU.add, ALU.mult), "h")
                elif slot == 6:
                    dve.wait_ge(*ge_act.after(i, "hi"))
                    ge_dve.inc(dve.scalar_tensor_tensor(
                        yb_lo[:, bass.ds(i * 4, 4), :].rearrange("p t n -> p (t n)"), SA, 0.5,
                        yb_hi[:, bass.ds(i * 4, 4), :].rearrange("p t n -> p (t n)").bitcast(F32),
                        ALU.mult, ALU.subtract), "lo")
                    ge_dve.end()

            run(stage["sz"], sz_evac, work=gelu)

            def glu_evac(i, g, n, done):
                if g == 0:
                    return
                if n == 0:
                    gl_dve.begin()
                    dve.wait_ge(*gl_act.units(i))
                dve.wait_ge(s_evac[1], stage["glu"].pair(i, 1) * 2 + (n + 3))
                dve.scalar_tensor_tensor(val[:, n * L:(n + 1) * L], gate[:, n * L:(n + 1) * L], 1.0,
                                         acc[:, n, 0:GC], ALU.add, ALU.mult).then_inc(s_evac[0], 1)

            def glu_work(i, slot):
                if slot == 3:
                    dve.wait_ge(s_evac[0], stage["glu"].pair(i, 0) * 2 + 4)
                    gl_dve.inc(dve.tensor_tensor(val, val, sz_gate[:, bass.ds(i * 512, 512)], ALU.mult), "w")
                    dve.wait_ge(*gl_act.after(i, "hi"))
                    gl_dve.inc(dve.scalar_tensor_tensor(
                        ya_lo[:, bass.ds(i * 2, 2), :].rearrange("p t n -> p (t n)"), val, 0.25,
                        ya_hi[:, bass.ds(i * 2, 2), :].rearrange("p t n -> p (t n)").bitcast(F32),
                        ALU.mult, ALU.subtract), "lo")
                    gl_dve.end()

            run(stage["glu"], glu_evac, work=glu_work)
            run(stage["merge_ssm"], merge_evac("merge_ssm"))
            mg_dve.begin()
            for c in range(4):
                dve.wait_ge(*mg_act.after(0, "hi", c))
                mg_dve.inc(dve.scalar_tensor_tensor(
                    m_lo[:, 4 * c:4 * c + 4, :].rearrange("p t n -> p (t n)"), merged[:, c * 1024:(c + 1) * 1024], 0.5,
                    m_hi[:, 4 * c:4 * c + 4, :].rearrange("p t n -> p (t n)").bitcast(F32),
                    ALU.mult, ALU.subtract), "lo")
            dve.wait_ge(s_xres, 16)

            def out_evac(i, g, n, done):
                dve.wait_ge(*done)
                o = mem_rows[:, n, bass.ds(i * 512 + g * GC, GC)]
                dve.tensor_tensor(o, acc[:, 2 * (g % 2) + n, 0:GC], o, ALU.add).then_inc(s_evac[g % 2], 1)

            run(stage["out"], out_evac, ends=True)

        @block.gpsimd
        def _(pool):
            pool.sem_inc(ss_pool.sem, ss_pool.base)
            pool.wait_ge(*prm_dve.units(1))
            sp_pool.begin()
            link = lambda ins, name: sp_pool.link(pool, ins, name, 0)

            def exp(x_, k, p, t, name):
                ts, tt = pool.tensor_scalar, pool.tensor_tensor
                link(ts(x_, x_, -88.0, 89.0, ALU.max, ALU.min), name)
                link(ts(k, x_, 1.4426950408889634, ROUND, ALU.mult, ALU.add), name)
                link(ts(k, k, -ROUND, None, ALU.add), name)
                for c in (-0.693359375, 2.12194440e-4):
                    link(ts(t, k, c, None, ALU.mult), name)
                    link(tt(x_, x_, t, ALU.add), name)
                link(ts(p, x_, 1.0 / 5040, 1.0 / 720, ALU.mult, ALU.add), name)
                for c in (1.0 / 120, 1.0 / 24, 1.0 / 6, 0.5, 1.0):
                    link(tt(p, p, x_, ALU.mult), name)
                    link(ts(p, p, c, None, ALU.add), name)
                link(tt(p, p, x_, ALU.mult), name)
                link(ts(p, p, 1.0, None, ALU.add), name)
                link(ts(t.bitcast(I32), k, 127.0, 8388608.0, ALU.add, ALU.mult), name)
                link(tt(x_, p, t, ALU.mult), name)

            pool.wait_ge(s_lam, 4 * 16)
            dt = spt("dt")[:, 0:2]
            exp(dt, spt("k")[:, 0:2], spt("p")[:, 0:2], spt("t")[:, 0:2], "dt")
            for a in range(2):
                h = slice(a * STATES, (a + 1) * STATES)
                link(pool.tensor_scalar(spt("mag")[:, h], spt("lr")[:, h], dt[:, a:a + 1], None, ALU.mult), "mag")
            exp(spt("mag"), spt("k"), spt("p"), spt("t"), "mag")
            for a in range(2):
                h = slice(a * STATES, (a + 1) * STATES)
                link(pool.tensor_scalar(spt("frac")[:, h], spt("li")[:, h], dt[:, a:a + 1], None, ALU.mult), "frac")
            link(pool.tensor_scalar(spt("k"), spt("frac"), 1.0 / TWO_PI, ROUND, ALU.mult, ALU.add), "frac")
            link(pool.tensor_scalar(spt("k"), spt("k"), -ROUND, None, ALU.add), "frac")
            c1 = 6.28125
            c2 = float(np.float32(np.round((TWO_PI - c1) * 2 ** 22) / 2 ** 22))
            for c in (c1, c2, TWO_PI - c1 - c2):
                link(pool.tensor_scalar(spt("t"), spt("k"), -c, None, ALU.mult), "frac")
                link(pool.tensor_tensor(spt("frac"), spt("frac"), spt("t"), ALU.add), "frac")
            link(pool.tensor_scalar(spt("frac"), spt("frac"), 1.0 / TWO_PI, None, ALU.mult), "frac")
            tt = lambda o, a, b, op, name: link(pool.tensor_tensor(spt(o), spt(a), spt(b), op), name)
            tt("den", "lr", "lr", ALU.mult, "den")
            tt("t", "li", "li", ALU.mult, "den")
            tt("den", "den", "t", ALU.add, "den")
            pool.wait_ge(*sp_act.after(0, "sin"))
            tt("hs", "hs", "hs", ALU.mult, "ab")
            link(pool.tensor_scalar(spt("hs"), spt("hs"), -2.0, 1.0, ALU.mult, ALU.add), "ab")
            tt("p", "mag", "hs", ALU.mult, "ab")
            tt("sn", "mag", "sn", ALU.mult, "ab")
            link(pool.tensor_scalar(spt("p"), spt("p"), -1.0, None, ALU.add), "ab")
            pool.wait_ge(*sp_dve.after(0, "rden"))
            tt("t", "p", "lr", ALU.mult, "f")
            tt("k", "sn", "li", ALU.mult, "f")
            tt("t", "t", "k", ALU.add, "f")
            tt("fr", "t", "den", ALU.mult, "f")
            tt("t", "sn", "lr", ALU.mult, "f")
            tt("k", "p", "li", ALU.mult, "f")
            tt("t", "t", "k", ALU.subtract, "f")
            tt("fi", "t", "den", ALU.mult, "f")
            sp_pool.end()

            pool.wait_ge(s_evac[1], 2 * (stage["conv"].group0 // 2) + 2)
            pool.wait_ge(s_evac[0], 2 * (stage["conv"].group0 // 2) + 2)
            with pool.Fori(0, 4) as i:
                ma_pool.begin()
                gate_on(pool, *ma_pe.units(i))
                qi = mq[:, bass.ds(i * (2 * L), 2 * L)]
                ma_pool.inc(pool.tensor_copy(ma_q, qi), "q")
                ma_pool.inc(pool.tensor_tensor(ma_sq, qi, qi, ALU.mult), "sq")
                ma_pool.inc(pool.tensor_copy(ma_v.rearrange("p (r n) -> p r n", r=RT),
                                             kv_rows[:, :, bass.ds(i * MHD + W, MHD)]), "v")
                ma_pool.end()

            pool.wait_ge(s_bc, 6 * 16)
            pool.wait_ge(*sp_act.after(0, "copy"))
            bb_pool.begin()
            f_of = lambda c: ssm_t[:, 32 * c:32 * (c + 1)].rearrange("p (t a) -> p t a", a=1).broadcast_to([P, 32, GH])
            as3 = lambda b: b.rearrange("p (t h) -> p t h", h=GH)
            bg, bv = as3(gate), as3(val)
            pool.wait_ge(s_line, 16)
            bb_pool.inc(pool.tensor_tensor(bg, ssm_b[:, 1], f_of(3), ALU.mult), "prod")
            bb_pool.inc(pool.tensor_tensor(bv, ssm_b[:, 0], f_of(3), ALU.mult), "prod")
            pool.wait_ge(*bb_pool.after(0, "prod", 1))
            bb_pool.inc(pool.tensor_tensor(ssm_b[:, 0], ssm_b[:, 0], f_of(2), ALU.mult), "prod")
            bb_pool.inc(pool.tensor_tensor(ssm_b[:, 1], ssm_b[:, 1], f_of(2), ALU.mult), "prod")
            pool.wait_ge(*bb_pool.after(0, "prod"))
            bb_pool.inc(pool.tensor_tensor(ssm_b[:, 0], ssm_b[:, 0], bg, ALU.subtract), "sum")
            bb_pool.inc(pool.tensor_tensor(ssm_b[:, 1], ssm_b[:, 1], bv, ALU.add), "sum")
            pool.wait_ge(*bb_pool.after(0, "sum"))
            pool.memset(sw_q[HD:P, 0, :], 0.0).then_inc(s_qpad, 1)
            pool.wait_ge(s_qpad, 1)
            pool.memset(sw_q[0:HD, 1, :], 0.0).then_inc(s_qpad, 1)
            pool.wait_ge(s_evac[0], 2 * (stage["akv"].group0 // 2) + 2)
            pool.wait_ge(s_evac[1], 2 * (stage["az"].group0 // 2) + 2)
            pool.wait_ge(s_qpad, 2)
            with pool.Fori(0, 4) as i:
                for sub in range(2):
                    t = i * 2 + sub
                    sw_pool.begin()
                    gate_on(pool, *sw_qk.units(t))
                    for e in range(2):
                        h = slice(e * HD, (e + 1) * HD)
                        sw_pool.inc(pool.tensor_copy(sw_q[h, e, :], aq[h, bass.ds(t * L, L)]), "q")
                        gate_on(pool, *sw_pool.after(t, "q", e))
                    q = aq[:, bass.ds(t * L, L)]
                    sw_pool.inc(pool.tensor_tensor(sw_sq, q, q, ALU.mult), "sq")
                    gate_on(pool, *st_pe.units(t))
                    sw_pool.inc(pool.tensor_copy(sw_v[:, :, :], v_rows[:, :, bass.ds(i * HD, HD)]), "v")
                    sw_pool.end()

            pool.wait_ge(*at_dve.units(1))
            with pool.Fori(0, 8) as n:
                ss_pool.begin()
                for c in range(2):
                    bt = ssm_b[:, c, bass.ds(n * 4, 4), :].rearrange("p (s a) h -> p s a h", a=1)
                    ss_pool.inc(pool.tensor_tensor(
                        masked_b[:, c * 512:(c + 1) * 512].rearrange("p (s j h) -> p s j h", s=4, j=8),
                        bt.broadcast_to([P, 4, 8, GH]),
                        state_group.rearrange("p s (j a) -> p s j a", a=1).broadcast_to([P, 4, 8, GH]), ALU.mult), "mask")
                for c in range(2):
                    ct = ssm_c[:, c, bass.ds(n, 1), :]
                    ss_pool.inc(pool.tensor_tensor(
                        masked_c[:, c * 512:(c + 1) * 512].rearrange("p (j n) -> p j n", j=8), ct.broadcast_to([P, 8, STATES]),
                        channel_group.rearrange("p (j a) -> p j a", a=1).broadcast_to([P, 8, STATES]), ALU.mult), "mask")
                def link(ins, name):
                    ss_pool.inc(ins, name)
                    gate_on(pool, ss_pool.sem, n * ss_pool.per + (ss_pool.base + ss_pool.k))

                th = ssm_t[:, bass.ds(n * 4 + 32, 4)].rearrange("p (s a) -> p s a", a=1).broadcast_to([P, 4, L])
                tm = time.rearrange("p (a n) -> p a n", a=1).broadcast_to([P, 4, L])
                ss_pool.inc(pool.tensor_tensor(phase.rearrange("p (s n) -> p s n", s=4), th, tm, ALU.mult), "ph")
                gate_on(pool, *ss_dve.after(n, "pre", 1))
                ss_pool.inc(pool.tensor_tensor(SA, SA, SB, ALU.add), "z")
                gate_on(pool, *ss_dve.after(n, "pre"))
                ss_pool.inc(pool.tensor_tensor(SE, SE, SH, ALU.subtract), "z")
                gate_on(pool, *ss_dve.after(n, "scan", 3))
                ss_pool.inc(pool.tensor_tensor(SA, SF, SB, ALU.mult), "x")
                gate_on(pool, *ss_dve.after(n, "scan"))
                link(pool.tensor_tensor(SE, SG, SH, ALU.mult), "x")
                ss_pool.inc(pool.tensor_tensor(SA, SA, SE, ALU.subtract), "x")
                ss_pool.end()

            o = out[0].rearrange("(r p) n -> p r n", p=P)
            st = stage["out"]
            with pool.Fori(0, st.turns) as i:
                gate_on(pool, s_evac[0], st.pair(i, 0) * 2 + 4)
                gate_on(pool, s_evac[1], st.pair(i, 1) * 2 + 4)
                pool.dma_start(o[:, :, bass.ds(i * 512, 512)], mem_rows[:, :, bass.ds(i * 512, 512)]).then_inc(s_out, 16)
            pool.wait_ge(s_out, 16 * st.turns)


_INS = ['x', 'mem', 'norm_g', 'mem_norm_g', 'w_in', 'lam_re', 'lam_im', 'log_dt', 'b_re', 'b_im', 'c_re', 'c_im',
        'd_skip', 'w_glu', 'conv_w', 'attn_q_g', 'attn_k_g', 'sinks', 'rel_bias', 'w_mem_kv', 'mem_q_g', 'mem_k_g',
        'w_branch', 'w_merge', 'b_merge', 'w_out']


def kernel(**inputs):
    import concourse.bacc as bacc
    from concourse.bass_utils import run_bass_kernel_spmd

    nc = bacc.Bacc("TRN2", target_bir_lowering=False, num_devices=1)
    arrays, args = {}, []
    given = [(n, np.ascontiguousarray(inputs[n])) for n in _INS]
    given += list(zip(["const_block", "const_onehot"], constants()))
    for name, a in given:
        arrays[f"in_{name}"] = a
        args.append(nc.dram_tensor(f"in_{name}", a.shape, mybir.dt.from_np(a.dtype), kind="ExternalInput").ap())
    args.append(nc.dram_tensor("out_0", (1, L, D), F32, kind="ExternalOutput").ap())
    hybrid_block(nc, *args)
    r = run_bass_kernel_spmd(nc, [arrays], core_ids=[0])
    return r.results[0]["out_0"]
```

```python
from contextlib import ExitStack, contextmanager

import numpy as np

import concourse.bass as bass
from concourse import mybir

F32 = mybir.dt.float32
F32R = mybir.dt.float32r
I32 = mybir.dt.int32
ALU = mybir.AluOpType
ACT = mybir.ActivationFunctionType
AX = mybir.AxisListType

P = 128
D = 2048
L = 256
W = 1024
KT = D // P
WT = W // P
RT = L // P
GC = 256
HK = 4
RING = 4
CHUNK = 64
HEADS = 16
KVH = 4
HD = 64
MHD = 256
STATES = 64
GH = 16
BUCKETS = 32
MAX_DISTANCE = 128
EPS = 1e-6
NEG = -1e30
WINDOW = 3 * CHUNK
LINE = 320
ROUND = 12582912.0
RSQRT_SEED = 1597463007.0
TWO_PI = 6.283185307179586
PI_BELOW = 3.1415925
GELU_C = 0.7978845608028654

COL_U, COL_SZ, COL_C, COL_AQ = 0, W, 2 * W, 6 * W
COL_AKV = COL_AQ + W
COL_AZ = COL_AKV + 2 * KVH * HD
COL_MQ = COL_AZ + W
PC_G, PC_MG, PC_BM, PC_D, PC_CONV = 0, KT, 2 * KT, 6 * KT, 6 * KT + WT


def t5_buckets(rel):
    nb = BUCKETS // 2
    max_exact = nb // 2
    sign = (rel > 0).astype(np.int32) * nb
    n = np.abs(rel)
    large = max_exact + (np.log(np.maximum(n, 1) / max_exact)
                         / np.log(MAX_DISTANCE / max_exact) * (nb - max_exact)).astype(np.int32)
    large = np.minimum(large, nb - 1)
    return (sign + np.where(n < max_exact, n, large)).astype(np.int32)


def constants():
    p = np.arange(P)
    ident = np.eye(P)
    channel_group = p[:, None] // GH == np.arange(8)[None, :]
    state_group = (np.arange(8)[None, None, :] == 2 * np.arange(4)[None, :, None] + p[:, None, None] // STATES)
    time = np.broadcast_to(np.arange(L) - L // 2, (P, L))
    head_ones = p[:, None] // HD == np.arange(2)[None, :]
    ones = np.ones((P, 2))
    block = np.concatenate([ident, channel_group, state_group.reshape(P, 32), time, head_ones, ones], 1)
    rel = np.arange(LINE) - (P - 1) - CHUNK
    onehot = t5_buckets(rel)[None, :] == np.arange(BUCKETS)[:, None]
    return block.astype(np.float32), onehot.astype(np.float32)


STATE_ROWS = ["lr", "li", "dt", "mag", "frac", "den", "sn", "hs", "fr", "fi"]
EXP_STEPS = 22
CONST_COLS = P + 8 + 32 + L + 2 + 2


class Stage:

    def __init__(self, name, turns, kts, half0, group0):
        self.name, self.turns, self.kts = name, turns, kts
        self.half0, self.group0 = half0, group0
        self.halves = sum(kts) // HK
        self.groups = len(kts)
        assert self.halves % RING == 0 and half0 % RING == 0 and self.groups % 2 == 0

    def half(self, turn, slot):
        return turn * self.halves + (self.half0 + slot)

    def pair(self, turn, g):
        return turn * (self.groups // 2) + (self.group0 + g) // 2


def plan():
    merge = [KT, WT, KT, WT]
    out, half, group = [], 0, 0
    for name, turns, kts in [
        ("km", 2, [KT] * 2), ("vm", 2, [KT] * 2), ("u", 2, [KT] * 2), ("mqz", 4, [KT] * 2),
        ("conv", 4, [KT] * 4), ("aq", 2, [KT] * 2), ("akv", 1, [KT] * 2), ("az", 2, [KT] * 2),
        ("merge_conv", 4, merge), ("merge_mem", 4, merge), ("merge_att", 4, merge),
        ("sz", 2, [KT] * 2), ("glu", 4, [WT] * 2), ("merge_ssm", 4, merge), ("out", 4, [KT] * 2),
    ]:
        st = Stage(name, turns, kts, half, group)
        out.append(st)
        half += turns * st.halves
        group += turns * st.groups
    return out


class Progress:

    def __init__(self, sem, steps, base=0):
        self.sem, self.steps, self.base = sem, steps, base
        self.per = sum(n for _, n in steps)
        self.k = 0

    def begin(self):
        self.k = 0

    def count(self, name, nth=None):
        c = 0
        for s, n in self.steps:
            if s == name:
                return c + (n if nth is None else nth + 1)
            c += n
        raise KeyError(name)

    def after(self, unit, name, nth=None):
        return self.sem, unit * self.per + (self.base + self.count(name, nth))

    def units(self, n):
        return self.sem, n * self.per + self.base

    def inc(self, ins, name):
        self.k += 1
        assert self.count(name) - dict(self.steps)[name] < self.k <= self.count(name), (name, self.k)
        return ins.then_inc(self.sem, 1)

    def link(self, eng, ins, name, unit):
        self.inc(ins, name)
        eng.wait_ge(self.sem, unit * self.per + (self.base + self.k))

    def end(self):
        assert self.k == self.per, (self.k, self.per)


@contextmanager
def turns_of(eng, n, first=0):
    if n - first == 1:
        yield first
    else:
        with eng.Fori(first, n) as i:
            yield i


def window_slots(head, tail):
    def work(i, slot):
        sub, s = slot // 6, slot % 6
        if sub or not isinstance(i, int):
            tail(i * 2 + (sub - 1), s)
        head(i, i * 2 + sub, s)
    return work


def hybrid_block(nc, x, mem, norm_g, mem_norm_g, w_in, lam_re, lam_im, log_dt, b_re, b_im, c_re, c_im,
                 d_skip, w_glu, conv_w, attn_q_g, attn_k_g, sinks, rel_bias, w_mem_kv, mem_q_g, mem_k_g,
                 w_branch, w_merge, b_merge, w_out, const_block, const_onehot, out):
    stages = plan()
    stage = {s.name: s for s in stages}
    ctx = ExitStack()
    with ctx:
        def sb(name, shape, dt=F32):
            return ctx.enter_context(nc.sbuf_tensor(name, shape, dt))

        def sem(name):
            return ctx.enter_context(nc.semaphore(name))

        x_hi = sb("x_hi", [P, KT, L], F32R)
        x_lo = sb("x_lo", [P, KT, L], F32R)
        raw = sb("raw", [P, RING, HK * GC])
        w_hi = sb("w_hi", [P, RING, HK * GC], F32R)
        w_lo = sb("w_lo", [P, RING, HK * GC], F32R)
        ya_hi = sb("ya_hi", [P, WT, L], F32R)
        ya_lo = sb("ya_lo", [P, WT, L], F32R)
        yb_hi = sb("yb_hi", [P, WT, L], F32R)
        yb_lo = sb("yb_lo", [P, WT, L], F32R)
        KB = 256
        region_at = nc.sbuf_base
        region = sb("region", [P, 32 * KB])
        assert nc.sbuf_base == region_at + 32 * 1024
        m_hi = nc.alloc_sbuf_tensor_at("m_hi", [P, KT, L], F32R, offset=region_at)
        m_lo = nc.alloc_sbuf_tensor_at("m_lo", [P, KT, L], F32R, offset=region_at + 16 * 1024)
        mq = region[:, 0:8 * KB]
        mz = region[:, 8 * KB:16 * KB]
        aq = region[:, 16 * KB:24 * KB]
        az = region[:, 24 * KB:32 * KB]
        arena = sb("arena", [P, 54 * KB])
        merged = arena[:, 0:16 * KB]
        B0 = 16

        def kb(lo, n):
            return arena[:, (B0 + lo) * KB:(B0 + lo + n) * KB]

        u = arena[:, 42 * KB:50 * KB]
        gate = arena[:, 50 * KB:52 * KB]
        val = arena[:, 52 * KB:54 * KB]
        mem_rows = merged.rearrange("p (r n) -> p r n", r=RT)
        x_flat = arena[:, (B0 + 18) * KB:(B0 + 34) * KB]
        x_rows = x_flat.rearrange("p (r n) -> p r n", r=RT)
        kv_rows = kb(0, 16).rearrange("p (r n) -> p r n", r=RT)
        km_t = merged[:, 0:8 * KB]
        cv = az.rearrange("p (g n) -> p g n", g=4)
        cv_th = kb(24, 2)
        ma_sq, ma_e, ma_pt, ma_sz = kb(16, 2), kb(18, 2), kb(20, 2), kb(22, 2)
        ma_q, ma_v = aq[:, 0:2 * KB], aq[:, 2 * KB:4 * KB]
        k_dup = kb(0, 4)
        v_rows = kb(4, 2).rearrange("p (r n) -> p r n", r=RT)
        bias_t = kb(6, 12).rearrange("p (h n) -> p h n", h=HEADS)
        sw_l = kb(18, 3).rearrange("p (w n) -> p w n", w=4)
        sw_e = kb(21, 4).rearrange("p (w n) -> p w n", w=4)
        sw_sq = kb(25, 1)
        sw_q = mq[:, 0:KB]
        sw_k = mq[:, KB:2 * KB]
        sw_pt = mq[:, 2 * KB:5 * KB].rearrange("p (e n) -> p e n", e=2)
        sw_sz = mq[:, 5 * KB:6 * KB]
        k_rows = kb(18, 2).rearrange("p (r n) -> p r n", r=RT)
        k_twice = kb(20, 4).rearrange("p (r k t n) -> p r k t n", r=RT, k=KVH, t=2)
        in_re, st_re = mq[:, 0:4 * KB], mq[:, 4 * KB:8 * KB]
        b_channels, c_states, in_im, cosines, sines, st_im = [kb(4 * n, 4) for n in range(6)]
        masked_b, masked_c = az[:, 0:4 * KB], az[:, 4 * KB:8 * KB]
        phase, whole = aq[:, 0:4 * KB], aq[:, 4 * KB:8 * KB]
        ssm_b = mz[:, 0:4 * KB].rearrange("p (c t h) -> p c t h", c=2, t=32)
        ssm_c = mz[:, 4 * KB:8 * KB].rearrange("p (c t n) -> p c t n", c=2, t=WT)
        sz_gate = aq

        const = sb("const", [P, CONST_COLS])
        ident = const[:, 0:P]
        channel_group = const[:, P:P + 8]
        state_group = const[:, P + 8:P + 40].rearrange("p (s j) -> p s j", s=4)
        time = const[:, P + 40:P + 40 + L]
        head_ones = const[:, P + 40 + L:P + 42 + L]
        ones = const[:, P + 42 + L:P + 44 + L]
        prm = sb("prm", [P, P])
        prm_t = sb("prm_t", [P, P])
        gain = sb("gain", [6, P])
        gain_t = sb("gain_t", [P, 8])
        rb = sb("rb", [BUCKETS, HEADS])
        sink_all = sb("sink_all", [P, HEADS])
        stat = sb("stat", [P, 96])
        ssm_t = sb("ssm_t", [P, 4 * 32])
        onehot = gate[0:BUCKETS, 0:LINE]
        line = val[0:HEADS, 0:LINE]
        line_dram = nc.dram_tensor("line_dram", (HEADS, P, LINE), F32, kind="Internal").ap()
        sw_v = sb("sw_v", [P, RT, HD])
        sp_buf = sb("sp_buf", [32, len(STATE_ROWS) * P])

        def spt(name):
            if name in ("k", "p", "t"):
                n = ("k", "p", "t").index(name)
                return gate[0:32, n * P:(n + 1) * P]
            n = STATE_ROWS.index(name)
            return sp_buf[:, n * P:(n + 1) * P]

        acc = ctx.enter_context(nc.psum_tensor("acc", [P, 4, 512], F32))
        side = ctx.enter_context(nc.psum_tensor("side", [P, 4, 512], F32))
        side_flat = side[:, :, :].rearrange("p b n -> p (b n)")

        s_raw = [sem(f"s_raw{n}") for n in range(RING)]
        s_hi = sem("s_hi")
        s_lo = sem("s_lo")
        s_mm = sem("s_mm")
        s_evac = [sem("s_evac0"), sem("s_evac1")]
        s_pass = sem("s_pass")
        s_const = sem("s_const")
        s_prm = sem("s_prm")
        s_small = sem("s_small")
        s_lam = sem("s_lam")
        s_mem_in = [sem("s_mem_in0"), sem("s_mem_in1")]
        s_x_in = sem("s_x_in")
        s_line = sem("s_line")
        s_bias = sem("s_bias")
        s_bc = sem("s_bc")
        s_xres = sem("s_xres")
        s_out = sem("s_out")
        s_neg = sem("s_neg")
        s_sum = sem("s_sum")
        norm_act = Progress(sem("norm_act"), [("hi", KT), ("ss", 2)])
        norm_dve = Progress(sem("norm_dve"), [("lo", KT), ("rs", 11)])
        norm_pe = Progress(sem("norm_pe"), [("tr", KT // 2)])
        xn_act = Progress(sem("xn_act"), [("ss", 1)])
        xn_dve = Progress(sem("xn_dve"), [("rs", 11), ("scale", 1)], base=1)
        xp_act = Progress(sem("xp_act"), [("hi", KT)])
        xp_dve = Progress(sem("xp_dve"), [("lo", KT)])
        xp_pe = Progress(sem("xp_pe"), [("tr", KT // 2)])
        prm_pe = Progress(sem("prm_pe"), [("tr", 1), ("line", 1)])
        prm_dve = Progress(sem("prm_dve"), [("copy", 3), ("gain", 1), ("gains", 2), ("line", 1)])
        kp_act = Progress(sem("kp_act"), [("ss", 8)])
        kp_dve = Progress(sem("kp_dve"), [("rs", 11), ("scale", 8), ("kmt", 2)])
        kp_pe = Progress(sem("kp_pe"), [("tr", 1)])
        ak_act = Progress(sem("ak_act"), [("ss", 8)])
        ak_dve = Progress(sem("ak_dve"), [("rs", 11), ("scale", 8), ("kt", 1)])
        ak_pe = Progress(sem("ak_pe"), [("tr", 1)])
        sp_pool = Progress(sem("sp_pool"), [("dt", EXP_STEPS), ("mag", 2 + EXP_STEPS), ("frac", 11),
                                            ("den", 3), ("ab", 5), ("f", 8)])
        sp_act = Progress(sem("sp_act"), [("sin", 2), ("copy", 1)])
        sp_dve = Progress(sem("sp_dve"), [("rden", 1)])
        sp_pe = Progress(sem("sp_pe"), [("tr", 1)])
        bb_pool = Progress(sem("bb_pool"), [("prod", 4), ("sum", 2)])
        cv_act = Progress(sem("cv_act"), [("th", 2), ("hi", 1)])
        cv_dve = Progress(sem("cv_dve"), [("v", 1), ("acc", 6), ("y", 1), ("sz", 1), ("yz", 1), ("lo", 1)], base=1)
        ma_pool = Progress(sem("ma_pool"), [("q", 1), ("sq", 1), ("v", 1)])
        ma_pe = Progress(sem("ma_pe"), [("qk", 1), ("tr", 1), ("pv", 1)], base=1)
        ma_dve = Progress(sem("ma_dve"), [("rs", 11), ("sc", 1), ("mx", 1), ("nb", 1), ("rsum", 1), ("p", 2),
                                          ("sz", 1), ("y", 1), ("lo", 1)], base=1)
        ma_act = Progress(sem("ma_act"), [("exp", 2), ("th", 1), ("pt", 1), ("hi", 1)], base=1)
        sw_pool = Progress(sem("sw_pool"), [("q", 1), ("sq", 1), ("k", 1), ("v", 1)])
        sw_qk = Progress(sem("sw_qk"), [("qk", 1)], base=1)
        sw_dve = Progress(sem("sw_dve"), [("rs", 11), ("sc", 1), ("l", 4), ("mx", 2), ("nb", 1), ("ds", 1),
                                          ("sum", 1), ("rsum", 1), ("p", 1)])
        sw_act = Progress(sem("sw_act"), [("exp", 4), ("es", 1)])
        st_pe = Progress(sem("st_pe"), [("tr", 1), ("pv", 1)], base=1)
        st_act = Progress(sem("st_act"), [("th", 1), ("pt", 2)])
        st_dve = Progress(sem("st_dve"), [("sz", 1), ("y", 1)], base=1)
        ss_pool = Progress(sem("ss_pool"), [("mask", 4), ("ph", 1), ("z", 2), ("x", 3)], base=1)
        ss_pe = Progress(sem("ss_pe"), [("tr", 1), ("bu", 1), ("y", 1)], base=1)
        ss_act = Progress(sem("ss_act"), [("bt", 1), ("ct", 1), ("sn", 1), ("hs", 1), ("sq", 1)], base=1)
        ss_dve = Progress(sem("ss_dve"), [("ph", 2), ("c", 1), ("pre", 4), ("scan", 8), ("szr", 1), ("czi", 1), ("xi", 1),
                                          ("ys", 1)], base=1)
        at_act = Progress(sem("at_act"), [("hi", 2)])
        at_dve = Progress(sem("at_dve"), [("lo", 2)])
        ge_act = Progress(sem("ge_act"), [("sq", 1), ("th", 1), ("hi", 1)])
        ge_dve = Progress(sem("ge_dve"), [("a", 2), ("h", 1), ("lo", 1)], base=1)
        zz_act = Progress(sem("zz_act"), [("th", 2)])
        zz_dve = Progress(sem("zz_dve"), [("sz", 2)], base=1)
        gl_act = Progress(sem("gl_act"), [("hi", 1)], base=1)
        gl_dve = Progress(sem("gl_dve"), [("w", 1), ("lo", 1)], base=1)
        mg_act = Progress(sem("mg_act"), [("hi", 2)])
        mg_dve = Progress(sem("mg_dve"), [("lo", 2)])

        def gate_on(eng, s, value):
            eng.wait_ge(s, value)
            eng.sem_inc(s_pass, 1)

        g_in = w_in[0]
        g_kv = w_mem_kv[0]

        def weights(st, turn, g):
            if st.name == "km":
                return g_kv, turn * 512 + g * GC
            if st.name == "vm":
                return g_kv, turn * 512 + (W + g * GC)
            if st.name == "u":
                return g_in, turn * 512 + (COL_U + g * GC)
            if st.name == "sz":
                return g_in, turn * 512 + (COL_SZ + g * GC)
            if st.name == "mqz":
                return g_in, turn * 512 + (COL_MQ + g * GC)
            if st.name == "conv":
                return g_in, turn * GC + (COL_C + g * W)
            if st.name == "aq":
                return g_in, turn * 512 + (COL_AQ + g * GC)
            if st.name == "akv":
                return g_in, COL_AKV + g * GC
            if st.name == "az":
                return g_in, turn * 512 + (COL_AZ + g * GC)
            if st.name == "glu":
                return w_glu[0], turn * GC + g * W
            if st.name == "out":
                return w_out[0], turn * 512 + g * GC
            b = ["merge_ssm", "merge_conv", "merge_att", "merge_mem"].index(st.name)
            return (w_merge if g % 2 == 0 else w_branch)[0, b], turn * 512 + (g // 2) * GC

        block = ctx.enter_context(nc.Block())

        @block.sync
        def _(sp):
            mem_r = mem[0].rearrange("(r p) n -> p r n", p=P)
            half_cols = D // 2
            sp.dma_start(mem_rows[:, :, 0:half_cols], mem_r[:, :, 0:half_cols]).then_inc(s_mem_in[0], 16)
            for at, rows in [
                (PC_G, norm_g.rearrange("a (t p) -> (a t) p", p=P)),
                (PC_MG, mem_norm_g.rearrange("a (t p) -> (a t) p", p=P)),
                (PC_BM, b_merge.rearrange("a b (t p) -> (a b t) p", p=P)),
                (PC_D, d_skip.rearrange("a (t p) -> (a t) p", p=P)),
                (PC_CONV, conv_w.rearrange("a b (t p) -> (a b t) p", p=P)),
            ]:
                sp.dma_start(prm[at:at + rows.shape[0], :], rows).then_inc(s_prm, 16)

            def load(st, i, slot, g, k):
                mat, col = weights(st, i, g)
                gate_on(sp, s_lo, st.half(i, slot + 1))
                src = mat[k * P:(k + HK) * P, bass.ds(col, GC)]
                sp.dma_start(raw[:, slot % RING, :].rearrange("p (k n) -> p k n", k=HK),
                             src.rearrange("(k p) n -> p k n", p=P)).then_inc(s_raw[slot % RING], 16)

            def turn(st, i, skip=0):
                slot = 0
                for g, kt in enumerate(st.kts):
                    for k in range(0, kt, HK):
                        if slot >= skip:
                            load(st, i, slot, g, k)
                        if skip and slot == RING - 1:
                            sp.dma_start(x_rows, x[0].rearrange("(r p) n -> p r n", p=P)).then_inc(s_x_in, 16)
                        slot += 1

            load(stages[0], 0, 0, 0, 0)
            sp.dma_start(mem_rows[:, :, half_cols:D], mem_r[:, :, half_cols:D]).then_inc(s_mem_in[1], 16)
            turn(stages[0], 0, skip=1)
            with turns_of(sp, stages[0].turns, 1) as i:
                turn(stages[0], i)
            for st in stages[1:]:
                with turns_of(sp, st.turns) as i:
                    turn(st, i)
            o = out[0].rearrange("(r p) n -> p r n", p=P)
            st = stage["out"]
            with sp.Fori(0, st.turns) as i:
                for g in range(2):
                    gate_on(sp, s_evac[g], st.pair(i, g) * 2 + 4)
                    sp.dma_start(o[:, :, bass.ds(i * 512 + g * GC, GC)],
                                 x_rows[:, :, bass.ds(i * 512 + g * GC, GC)]).then_inc(s_out, 16)
            sp.wait_ge(s_out, 16 * 2 * st.turns)

        @block.tensor
        def _(pe):
            def half_products(st, i, slot, g, k0, kts, hi, lo, rows):
                r = slot % RING
                pe.wait_ge(s_lo, st.half(i, slot + 1 + RING))
                for n in range(2):
                    if k0 == 0:
                        pe.wait_ge(s_evac[g % 2], st.pair(i, g) * 2 + (n + 1))
                    for k in range(HK):
                        kk = k0 + k
                        o = acc[:, 2 * (g % 2) + n, 0:GC]
                        first, final = kk == 0, kk == kts - 1
                        if rows:
                            a_hi, a_lo = hi[:, kk, n * P:(n + 1) * P], lo[:, kk, n * P:(n + 1) * P]
                            b_hi, b_lo = w_hi[:, r, k * GC:(k + 1) * GC], w_lo[:, r, k * GC:(k + 1) * GC]
                            pe.matmul(o, a_hi, b_hi, start=first, stop=False)
                            pe.matmul(o, a_hi, b_lo, start=False, stop=False)
                            last = pe.matmul(o, a_lo, b_hi, start=False, stop=final)
                        else:
                            c = k * GC + n * P
                            a_hi, a_lo = w_hi[:, r, c:c + P], w_lo[:, r, c:c + P]
                            b_hi, b_lo = hi[:, kk, :], lo[:, kk, :]
                            pe.matmul(o, a_hi, b_hi, start=first, stop=False)
                            pe.matmul(o, a_hi, b_lo, start=False, stop=False)
                            last = pe.matmul(o, a_lo, b_hi, start=False, stop=final)
                    last.then_inc(s_mm, 1)

            def run(st, operands, rows=False, work=None, ready=None, peel=False):
                def turn(i):
                    slot = 0
                    for g, kts in enumerate(st.kts):
                        hi, lo = operands(g)
                        for k0 in range(0, kts, HK):
                            if ready:
                                ready(i, g, k0)
                            half_products(st, i, slot, g, k0, kts, hi, lo, rows)
                            if work:
                                work(i, slot)
                            slot += 1

                if peel:
                    turn(0)
                with turns_of(pe, st.turns, int(peel)) as i:
                    turn(i)

            def bank_of_transposes(pr, after, rows, b):
                if b >= 4:
                    pe.wait_ge(*after.after(0, "lo", 2 * (b - 4) + 1))
                for kt in (2 * b, 2 * b + 1):
                    for r in range(RT):
                        c = (kt % 8) * L + r * P
                        last = pe.transpose(side_flat[:, c:c + P], rows[:, r, kt * P:(kt + 1) * P], ident)
                pr.inc(last, "tr")

            xs = lambda g: (x_hi, x_lo)
            ms = lambda g: (m_hi, m_lo)
            pe.sem_inc(s_mm, 2 * RING)
            for pr in (ma_pe, sw_qk, st_pe, ss_pe):
                pe.sem_inc(pr.sem, pr.base)
            pe.wait_ge(s_const, 16)
            pe.wait_ge(s_prm, 5 * 16)
            prm_pe.begin()
            prm_pe.inc(pe.transpose(side[:, 0, 0:P], prm[:, :], ident), "tr")
            pe.wait_ge(*prm_dve.after(0, "copy"))
            pe.wait_ge(s_mem_in[0], 16)
            norm_pe.begin()
            for b in range(4):
                bank_of_transposes(norm_pe, norm_dve, mem_rows, b)

            def memory_transposes(i, slot):
                if i == 0 and slot < 2:
                    pe.wait_ge(s_mem_in[1], 16)
                    for b in (4 + 2 * slot, 5 + 2 * slot):
                        bank_of_transposes(norm_pe, norm_dve, mem_rows, b)

            def memory_ready(i, g, k0):
                if g == 0:
                    pe.wait_ge(*norm_dve.after(0, "lo", k0 + HK - 1))

            run(stage["km"], ms, rows=True, ready=memory_ready, work=memory_transposes, peel=True)
            pe.wait_ge(s_small, 8 * 16)
            pe.wait_ge(*xn_act.units(2))
            pe.matmul(side[0:HEADS, 1, 0:LINE], rb[:, :], onehot, start=True, stop=True)
            prm_pe.inc(pe.transpose(side[:, 0, P:P + 6], gain[:, :], ident[0:6, 0:6]), "line")

            def x_transposes(i, slot):
                if i == 0:
                    if slot == 0:
                        xp_pe.begin()
                        pe.wait_ge(*prm_dve.units(1))
                        pe.wait_ge(*xn_dve.units(2))
                    bank_of_transposes(xp_pe, xp_dve, x_rows, slot)

            run(stage["vm"], ms, rows=True, work=x_transposes, peel=True)
            pe.wait_ge(*xp_dve.units(1))
            pe.wait_ge(*kp_dve.after(0, "scale"))
            for f in range(WT):
                for r in range(RT):
                    last = pe.transpose(side_flat[:, f * L + r * P:f * L + (r + 1) * P],
                                        kv_rows[:, r, f * P:(f + 1) * P], ident)
            kp_pe.begin()
            kp_pe.inc(last, "tr")
            run(stage["u"], xs)
            run(stage["mqz"], xs)
            pe.wait_ge(*sp_pool.units(1))
            pe.wait_ge(*kp_dve.units(1))
            for n, c in enumerate(["mag", "frac", "fr", "fi"]):
                last = pe.transpose(side[:, 0, n * 32:(n + 1) * 32], spt(c), ident[0:32, 0:32])
            sp_pe.begin()
            sp_pe.inc(last, "tr")

            def mem_attention(i, slot):
                if slot == 1:
                    ma_pe.begin()
                    pe.wait_ge(*ma_pool.after(i, "v"))
                    pe.wait_ge(*sp_act.units(1))
                    pe.wait_ge(*ma_dve.units(i))
                    pe.wait_ge(*ma_act.units(i))
                    for r in range(RT):
                        for t in range(2):
                            pe.matmul(side[:, 0, r:r + 1], ma_sq[:, t * L + r * P:t * L + (r + 1) * P], ones[:, 0:1],
                                      start=t == 0, stop=t == 1)
                    for r in range(RT):
                        for t in range(2):
                            last = pe.matmul(side[:, 1, r * L:(r + 1) * L], ma_q[:, t * L + r * P:t * L + (r + 1) * P],
                                             km_t[:, bass.ds(i * (2 * L) + t * L, L)], start=t == 0, stop=t == 1)
                    ma_pe.inc(last, "qk")
                elif slot == 9:
                    pe.wait_ge(*ma_dve.after(i, "p"))
                    for k in range(2):
                        for r in range(RT):
                            last = pe.transpose(side[:, 2, k * L + r * P:k * L + (r + 1) * P],
                                                ma_e[:, r * L + k * P:r * L + (k + 1) * P], ident)
                    ma_pe.inc(last, "tr")
                elif slot == 12:
                    pe.wait_ge(*ma_act.after(i, "pt"))
                    for f in range(2):
                        for k in range(2):
                            last = pe.matmul(side[:, 3, f * L:(f + 1) * L],
                                             ma_v[:, k * L + f * P:k * L + (f + 1) * P],
                                             ma_pt[:, k * L:(k + 1) * L], start=k == 0, stop=k == 1)
                    ma_pe.inc(last, "pv")
                    ma_pe.end()

            run(stage["conv"], xs, work=mem_attention)
            run(stage["aq"], xs)
            run(stage["akv"], xs, rows=True)
            run(stage["az"], xs)
            pe.wait_ge(*ak_dve.after(0, "scale"))
            pe.wait_ge(*ma_dve.units(4))
            for k in range(KVH):
                for r in range(RT):
                    last = pe.transpose(side_flat[:, k * L + r * P:k * L + (r + 1) * P],
                                        k_twice[:, r, k, :, :].rearrange("p t n -> p (t n)"), ident)
            ak_pe.begin()
            ak_pe.inc(last, "tr")

            def window_head(i, t, s):
                if s == 0:
                    sw_qk.begin()
                    pe.wait_ge(*sw_pool.after(t, "k"))
                    if not (isinstance(t, int) and t == 0):
                        pe.wait_ge(*sw_dve.after(t - 1, "l"))
                    for r in range(RT):
                        pe.matmul(side[:, 1 + r, WINDOW:WINDOW + 2], sw_sq[:, r * P:(r + 1) * P], head_ones,
                                  start=True, stop=True)
                    for e in range(2):
                        strip = slice(e * HD, (e + 1) * HD)
                        pe.matmul(side[:, 1 + e, CHUNK:WINDOW], sw_q[strip, 0:P], sw_k[strip, 0:P],
                                  start=True, stop=True)
                    for e in range(2):
                        strip = slice(e * HD, (e + 1) * HD)
                        last = pe.matmul(side[:, 1 + e, 256:256 + WINDOW], sw_q[strip, P:2 * P], sw_k[strip, CHUNK:L],
                                         start=True, stop=True)
                    sw_qk.inc(last, "qk")
                    sw_qk.end()

            def window_tail(t, s):
                if s == 1:
                    st_pe.begin()
                    pe.wait_ge(*sw_dve.after(t, "p"))
                    pe.wait_ge(*st_dve.units(t))
                    for e in range(2):
                        b = 3 if e == 0 else 0
                        pe.transpose(side[:, b, 0:P], sw_e[:, e, P:2 * P], ident)
                        pe.transpose(side[:, b, P:2 * P], sw_e[:, 2 + e, 0:P], ident)
                        last = pe.transpose(side[:, b, 2 * P:3 * P], sw_e[:, 2 + e, P:2 * P], ident)
                    st_pe.inc(last, "tr")
                elif s == 3:
                    pe.wait_ge(*st_act.after(t, "pt"))
                    pe.wait_ge(*sw_pool.after(t, "v"))
                    for e in range(2):
                        rows = slice(e * HD, (e + 1) * HD)
                        pe.matmul(side[rows, 3, 0:P], sw_v[:, 0, :], sw_pt[:, e, 0:P], start=True, stop=True)
                        pe.matmul(side[rows, 3, P:2 * P], sw_v[:, 0, :], sw_pt[:, e, P:2 * P], start=True, stop=False)
                        last = pe.matmul(side[rows, 3, P:2 * P], sw_v[:, 1, :], sw_pt[:, e, 2 * P:3 * P],
                                         start=False, stop=True)
                    st_pe.inc(last, "pv")
                    st_pe.end()

            def merge_operands(hi, lo):
                return lambda g: (x_hi, x_lo) if g % 2 == 0 else (hi, lo)

            def branch_ready(waits):
                def ready(i, g, k0):
                    if g == 1 and k0 == 0:
                        for w in waits:
                            pe.wait_ge(*w)
                return ready

            run(stage["merge_conv"], merge_operands(ya_hi, ya_lo), ready=branch_ready([cv_dve.units(4)]),
                work=window_slots(window_head, window_tail), peel=True)
            for s in range(6):
                window_tail(7, s)

            def state_space(first):
                def work(i, slot):
                    n = i + first
                    if slot == 0:
                        ss_pe.begin()
                        pe.wait_ge(*ss_pool.after(n, "mask"))
                        pe.wait_ge(*st_dve.units(8))
                        pe.wait_ge(*ss_dve.units(n))
                        pe.wait_ge(*ss_act.units(n))
                        for b, (src, c) in enumerate([(masked_b, 0), (masked_b, 512),
                                                          (masked_c, 0), (masked_c, 512)]):
                            for s in range(4):
                                last = pe.transpose(side[:, b, s * P:(s + 1) * P],
                                                    src[:, c + s * P:c + (s + 1) * P], ident)
                        ss_pe.inc(last, "tr")
                    elif slot == 2:
                        pe.wait_ge(*ss_act.after(n, "ct"))
                        for c in range(2):
                            for s in range(4):
                                last = pe.matmul(side[:, s, c * L:(c + 1) * L],
                                                 b_channels[:, c * 512 + s * P:c * 512 + (s + 1) * P],
                                                 u[:, bass.ds(n * L, L)], start=True, stop=True)
                        ss_pe.inc(last, "bu")
                    elif slot == 10:
                        pe.wait_ge(*ss_pool.after(n, "x"))
                        pe.wait_ge(*ss_dve.after(n, "xi"))
                        for c, x_ in enumerate([in_re, b_channels]):
                            for s in range(4):
                                strip = slice(32 * s, 32 * (s + 1))
                                o = c * 512 + s * P + 32 * s
                                last = pe.matmul(side[strip, 0, 0:L], c_states[:, o:o + 32], x_[:, s * L:(s + 1) * L],
                                                 start=c == 0, stop=c == 1)
                        ss_pe.inc(last, "y")
                        ss_pe.end()
                return work

            run(stage["merge_mem"], merge_operands(yb_hi, yb_lo), work=state_space(0),
                ready=branch_ready([ma_dve.units(4), st_dve.units(8)]))
            run(stage["merge_att"], merge_operands(ya_hi, ya_lo), work=state_space(4),
                ready=branch_ready([at_dve.units(1)]))
            run(stage["sz"], xs)

            def gelu_ready(i, g, k0):
                if g == 0:
                    pe.wait_ge(*ge_dve.units(k0 // HK + 1))

            run(stage["glu"], lambda g: (yb_hi, yb_lo), ready=gelu_ready)
            run(stage["merge_ssm"], merge_operands(ya_hi, ya_lo), ready=branch_ready([gl_dve.units(4)]))

            def merged_ready(i, g, k0):
                if g == 0:
                    pe.wait_ge(*mg_dve.units(k0 // HK + 1))

            run(stage["out"], ms, rows=True, ready=merged_ready)

        @block.scalar
        def _(act):
            for pr in (ma_act, ss_act, gl_act):
                act.sem_inc(pr.sem, pr.base)
            act.dma_start(const[:, :], const_block).then_inc(s_const, 16)

            def split(r, count, free):
                gate_on(act, s_raw[r], count)
                act.wait_ge(s_mm, free)
                act.activation(w_hi[:, r, :], raw[:, r, :], ACT.Copy).then_inc(s_hi, 1)

            def run(st, evac, work=None, ends=False, peel=False):
                def turn(i, last):
                    slot = 0
                    for g, kts in enumerate(st.kts):
                        for k in range(0, kts, HK):
                            if k == kts - HK and evac:
                                for n in range(2):
                                    evac(i, g, n, (s_mm, st.half(i, slot) * 2 + (n + 1 + 2 * RING)))
                            if not (last and slot + RING >= st.halves):
                                q = st.half(i, slot)
                                split(slot % RING, (i * (st.halves // RING) + (st.half0 + slot) // RING + 2) * 16,
                                      q * 2 + (2 + 2 * RING))
                            if work:
                                work(i, slot)
                            slot += 1
                if ends:
                    with turns_of(act, st.turns - 1) as i:
                        turn(i, False)
                    turn(st.turns - 1, True)
                else:
                    if peel:
                        turn(0, False)
                    with turns_of(act, st.turns, int(peel)) as i:
                        turn(i, False)

            def copy_to(dst, scale=lambda n: 1.0):
                def evac(i, g, n, done):
                    gate_on(act, *done)
                    act.activation(dst(i, g, n), acc[:, 2 * (g % 2) + n, 0:GC], ACT.Copy,
                                   scale=scale(n)).then_inc(s_evac[g % 2], 1)
                return evac

            def part(pr, tr, hi, col, kt):
                act.wait_ge(*tr.after(0, "tr", kt // 2))
                c = (kt % 8) * L
                pr.inc(act.activation(hi[:, kt, :], side_flat[:, c:c + L], ACT.Copy,
                                      scale=prm_t[:, col + kt:col + kt + 1]), "hi")

            norm_act.begin()
            for r in range(RING):
                for kt in range(HK * r, HK * (r + 1)):
                    part(norm_act, norm_pe, m_hi, PC_MG, kt)
                act.wait_ge(s_raw[r], 16)
                act.activation(w_hi[:, r, :], raw[:, r, :], ACT.Copy).then_inc(s_hi, 1)

            def row_sums(i, slot):
                if i == 0 and slot < RT:
                    act.wait_ge(s_mem_in[0], 16)
                    act.wait_ge(s_mem_in[1], 16)
                    norm_act.inc(act.activation(kb(0, 8), mem_rows[:, slot, :], ACT.Square,
                                                accum_out=stat[:, slot:slot + 1]), "ss")
                    act.wait_ge(*norm_act.after(0, "ss", slot))
                    if slot == RT - 1:
                        norm_act.end()
                elif slot == 4:
                    xn_act.begin()
                    act.wait_ge(s_x_in, 16)
                    gate_on(act, *xn_dve.units(i))
                    xn_act.inc(act.activation(side_flat, x_flat[:, bass.ds(i * D, D)], ACT.Square,
                                              accum_out=stat[:, 4:5]), "ss")
                    xn_act.end()

            def memory_scale(n):
                return stat[:, 2 + n:3 + n]

            km_copy = copy_to(lambda i, g, n: kv_rows[:, n, bass.ds(i * 512 + g * GC, GC)], memory_scale)

            def km_evac(i, g, n, done):
                if i == 0 and g == 0 and n == 0:
                    act.wait_ge(*norm_dve.units(1))
                km_copy(i, g, n, done)

            run(stage["km"], km_evac, work=row_sums, peel=True)
            act.wait_ge(*prm_dve.units(1))
            act.dma_start(line_dram, line.rearrange("h (a n) -> h a n", a=1).broadcast_to([HEADS, P, LINE]))\
               .then_inc(s_line, 16)
            act.wait_ge(s_evac[0], 2 + 4)
            act.wait_ge(s_evac[1], 2 + 4)
            kp_act.begin()
            for r in range(RT):
                for h in range(4):
                    kp_act.inc(act.activation(kb(16, 1), kv_rows[:, r, h * MHD:(h + 1) * MHD], ACT.Square,
                                              accum_out=stat[:, 8 + 4 * r + h:9 + 4 * r + h]), "ss")
                    act.wait_ge(*kp_act.after(0, "ss", 4 * r + h))

            def x_parts(i, slot):
                if i == 0:
                    if slot == 0:
                        xp_act.begin()
                    for kt in (2 * slot, 2 * slot + 1):
                        part(xp_act, xp_pe, x_hi, PC_G, kt)

            run(stage["vm"], copy_to(lambda i, g, n: kv_rows[:, n, bass.ds(i * 512 + (W + g * GC), GC)], memory_scale),
                work=x_parts, peel=True)
            run(stage["u"], copy_to(lambda i, g, n: u[:, bass.ds(i * 1024 + (2 * g + n) * L, L)]))
            act.wait_ge(*sp_pool.after(0, "frac"))
            sp_act.begin()
            sp_act.inc(act.activation(spt("sn"), spt("frac"), ACT.Sin, scale=2 * PI_BELOW), "sin")
            sp_act.inc(act.activation(spt("hs"), spt("frac"), ACT.Sin, scale=PI_BELOW), "sin")
            run(stage["mqz"], copy_to(lambda i, g, n: region[:, bass.ds(i * 1024 + (2 * g + n) * L, L)]))
            act.wait_ge(*sp_pe.after(0, "tr"))
            sp_act.inc(act.activation(ssm_t[:, :], side[:, 0, 0:P], ACT.Copy), "copy")

            def conv_evac(i, g, n, done):
                src = acc[:, 2 * (g % 2) + n, 0:GC]
                act.wait_ge(*done)
                if g == 3:
                    if n == 0:
                        cv_act.begin()
                    cv_act.inc(act.activation(cv_th[:, n * L:(n + 1) * L], src, ACT.Tanh, scale=0.5), "th")
                elif n == 0:
                    act.wait_ge(*cv_dve.units(i))
                act.activation(cv[:, g, n * L:(n + 1) * L], src, ACT.Copy).then_inc(s_evac[g % 2], 1)

            def conv_work(i, slot):
                mem_attention(i, slot)
                if slot == 15:
                    gate_on(act, *cv_dve.after(i, "yz"))
                    cv_act.inc(act.activation(ya_hi[:, bass.ds(i * 2, 2), :].rearrange("p t n -> p (t n)"),
                                              cv[:, 2, :], ACT.Copy, scale=0.5), "hi")
                    cv_act.end()

            def mem_attention(i, slot):
                if slot == 5:
                    ma_act.begin()
                    act.wait_ge(*ma_dve.after(i, "nb"))
                    for r in range(RT):
                        ma_act.inc(act.activation(ma_e[:, r * L:(r + 1) * L], side[:, 1, r * L:(r + 1) * L], ACT.Exp,
                                                  scale=stat[:, 34 + r:35 + r], bias=stat[:, 38 + r:39 + r],
                                                  accum_out=stat[:, 40 + r:41 + r]), "exp")
                    act.wait_ge(*ma_act.after(i, "exp"))
                    act.sem_inc(s_pass, 1)
                    ma_act.inc(act.activation(ma_sz, mz[:, bass.ds(i * (2 * L), 2 * L)], ACT.Tanh, scale=0.5), "th")
                elif slot == 10:
                    act.wait_ge(*ma_pe.after(i, "tr"))
                    ma_act.inc(act.activation(ma_pt, side[:, 2, :], ACT.Copy), "pt")
                elif slot == 13:
                    gate_on(act, *ma_dve.after(i, "y"))
                    ma_act.inc(act.activation(yb_hi[:, bass.ds(i * 2, 2), :].rearrange("p t n -> p (t n)"),
                                              ma_sz, ACT.Copy, scale=0.5), "hi")
                    ma_act.end()

            run(stage["conv"], conv_evac, work=conv_work)
            run(stage["aq"], copy_to(lambda i, g, n: aq[:, bass.ds(i * 1024 + (2 * g + n) * L, L)]))

            def akv_evac(i, g, n, done):
                act.wait_ge(*done)
                dst = (k_rows if g == 0 else v_rows)[:, n, :]
                act.activation(dst, acc[:, 2 * (g % 2) + n, 0:GC], ACT.Copy).then_inc(s_evac[g % 2], 1)

            run(stage["akv"], akv_evac)
            act.wait_ge(s_evac[0], 2 * (stage["az"].group0 // 2) + 2)
            ak_act.begin()
            for r in range(RT):
                for h in range(KVH):
                    ak_act.inc(act.activation(side[:, 0, 0:HD], k_rows[:, r, h * HD:(h + 1) * HD], ACT.Square,
                                              accum_out=stat[:, 16 + 4 * r + h:17 + 4 * r + h]), "ss")
                    act.wait_ge(*ak_act.after(0, "ss", 4 * r + h))
            act.wait_ge(s_line, 16)
            act.dma_start(bias_t, bass.AP(tensor=line_dram.tensor, offset=P - 1,
                                          ap=[[LINE - 1, P], [P * LINE, HEADS], [1, WINDOW]])).then_inc(s_bias, 16)
            for c, src in enumerate([b_re, b_im]):
                for a in range(2):
                    act.dma_start(ssm_b[a * STATES:(a + 1) * STATES, c, :, :],
                                  src[0].rearrange("(t a) p h -> a p t h", a=2)[a]).then_inc(s_bc, 16)
            for c, src in enumerate([c_re, c_im]):
                act.dma_start(ssm_c[:, c, :, :],
                              src[0].rearrange("(t g) h p -> (g h) t p", g=8)).then_inc(s_bc, 16)
            run(stage["az"], copy_to(lambda i, g, n: az[:, bass.ds(i * 1024 + (2 * g + n) * L, L)]))

            def gate_evac(name, b):
                def evac(i, g, n, done):
                    if g % 2:
                        return
                    act.wait_ge(*done)
                    gate_on(act, s_evac[1], stage[name].pair(i, g) * 2 + (n + 1))
                    act.activation(gate[:, n * L:(n + 1) * L], acc[:, n, 0:GC], ACT.Tanh, scale=0.5,
                                   bias=prm_t[:, bass.ds(i * 4 + (PC_BM + KT * b + g + n), 1)]).then_inc(s_evac[0], 1)
                return evac

            def window_head(i, t, s):
                if s == 2:
                    sw_act.begin()
                    act.wait_ge(*sw_dve.after(t, "ds"))
                    for w in range(4):
                        sw_act.inc(act.activation(sw_e[:, w, CHUNK:256], sw_l[:, w, :], ACT.Exp,
                                                  bias=stat[:, 60 + w:61 + w], accum_out=stat[:, 64 + w:65 + w]), "exp")
                    sw_act.inc(act.activation(stat[:, 72:76], stat[:, 68:72], ACT.Exp), "es")
                    sw_act.end()

            def window_tail(t, s):
                if s == 0:
                    st_act.begin()
                    gate_on(act, *st_dve.units(t))
                    st_act.inc(act.activation(sw_sz, az[:, bass.ds(t * L, L)], ACT.Tanh, scale=0.5), "th")
                elif s == 2:
                    act.wait_ge(*st_pe.after(t, "tr"))
                    for e in range(2):
                        st_act.inc(act.activation(sw_pt[:, e, :], side[:, 3 if e == 0 else 0, 0:3 * P], ACT.Copy), "pt")
                    st_act.end()

            act.wait_ge(*bb_pool.units(1))
            run(stage["merge_conv"], gate_evac("merge_conv", 1), work=window_slots(window_head, window_tail), peel=True)
            for s in range(6):
                window_tail(7, s)
            at_act.begin()
            act.wait_ge(*st_dve.units(8))
            act.wait_ge(s_mm, 2 * stage["merge_mem"].half0 + 2 * RING)
            for h in range(2):
                at_act.inc(act.activation(ya_hi[:, 4 * h:4 * h + 4, :].rearrange("p t n -> p (t n)"),
                                          aq[:, h * 1024:(h + 1) * 1024], ACT.Copy, scale=0.5), "hi")

            def state_space(first):
                def work(i, slot):
                    n = i + first
                    if slot == 0:
                        ss_act.begin()
                        act.wait_ge(*ss_pe.after(n, "tr"))
                        ss_act.inc(act.activation(b_channels, side_flat[:, 0:1024], ACT.Copy), "bt")
                        ss_act.inc(act.activation(c_states, side_flat[:, 1024:2048], ACT.Copy), "ct")
                    elif slot == 1:
                        act.wait_ge(*ss_dve.after(n, "ph"))
                        act.wait_ge(*ss_pool.units(n))
                        ss_act.inc(act.activation(sines, phase, ACT.Sin, scale=2 * PI_BELOW), "sn")
                        ss_act.inc(act.activation(cosines, phase, ACT.Sin, scale=PI_BELOW), "hs")
                        act.wait_ge(*ss_act.after(n, "hs"))
                        ss_act.inc(act.activation(cosines, cosines, ACT.Square), "sq")
                        ss_act.end()
                return work

            run(stage["merge_mem"], gate_evac("merge_mem", 3), work=state_space(0))
            run(stage["merge_att"], gate_evac("merge_att", 2), work=state_space(4))

            def sz_evac(i, g, n, done):
                act.wait_ge(*done)
                if n == 0:
                    gate_on(act, *zz_dve.units(i * 2 + g))
                if n == 0:
                    zz_act.begin()
                zz_act.inc(act.activation(gate[:, n * L:(n + 1) * L], acc[:, 2 * (g % 2) + n, 0:GC], ACT.Tanh,
                                          scale=0.5), "th")
                act.sem_inc(s_pass, 1)
                act.activation(sz_gate[:, bass.ds(i * 1024 + (2 * g + n) * L, L)], acc[:, 2 * (g % 2) + n, 0:GC],
                               ACT.Copy).then_inc(s_evac[g % 2], 1)
                if n == 1:
                    zz_act.end()

            def gelu(i, slot):
                ui = u[:, bass.ds(i * 1024, 1024)]
                if slot == 0:
                    ge_act.begin()
                    act.wait_ge(*ss_dve.units(8))
                    gate_on(act, *ge_dve.units(i))
                    ge_act.inc(act.activation(in_re, ui, ACT.Square), "sq")
                elif slot == 2:
                    act.wait_ge(*ge_dve.after(i, "a"))
                    ge_act.inc(act.activation(st_re, st_re, ACT.Tanh, scale=GELU_C), "th")
                elif slot == 5:
                    gate_on(act, *ge_dve.after(i, "h"))
                    ge_act.inc(act.activation(yb_hi[:, bass.ds(i * 4, 4), :].rearrange("p t n -> p (t n)"),
                                              in_re, ACT.Copy, scale=0.5), "hi")
                    ge_act.end()

            act.wait_ge(*at_dve.units(1))
            act.wait_ge(s_evac[1], 2 * (stage["sz"].group0 // 2) + 2)
            run(stage["sz"], sz_evac, work=gelu)

            def glu_evac(i, g, n, done):
                if g == 0:
                    return
                act.wait_ge(*done)
                if n == 0:
                    act.wait_ge(*gl_dve.units(i))
                act.activation(gate[:, n * L:(n + 1) * L], acc[:, 2 + n, 0:GC], ACT.Tanh, scale=0.5)\
                   .then_inc(s_evac[1], 1)

            def glu_work(i, slot):
                if slot == 3:
                    gl_act.begin()
                    gate_on(act, *gl_dve.after(i, "w"))
                    gl_act.inc(act.activation(ya_hi[:, bass.ds(i * 2, 2), :].rearrange("p t n -> p (t n)"),
                                              val, ACT.Copy, scale=0.25), "hi")
                    gl_act.end()

            act.wait_ge(*zz_dve.units(4))
            run(stage["glu"], glu_evac, work=glu_work)
            act.wait_ge(*gl_dve.units(4))
            act.dma_start(x_rows, x[0].rearrange("(r p) n -> p r n", p=P)).then_inc(s_xres, 16)

            def merged_parts(i, slot):
                if slot in (8, 11):
                    h = slot // 11
                    if h == 0:
                        mg_act.begin()
                    gate_on(act, s_sum, i * 4 + (2 * KT + 2 + 2 * h))
                    mg_act.inc(act.activation(m_hi[:, bass.ds(i * 4 + 2 * h, 2), :].rearrange("p t n -> p (t n)"),
                                              merged[:, bass.ds(i * 1024 + 512 * h, 512)], ACT.Copy, scale=0.5), "hi")

            run(stage["merge_ssm"], gate_evac("merge_ssm", 0), work=merged_parts)
            run(stage["out"], None, ends=True)

        @block.vector
        def _(dve):
            dve.sem_inc(s_lo, RING)
            dve.sem_inc(s_evac[0], 2)
            dve.sem_inc(s_evac[1], 2)
            for pr in (xn_dve, ma_dve, cv_dve, st_dve, ss_dve, ge_dve, zz_dve, gl_dve):
                dve.sem_inc(pr.sem, pr.base)

            def rest(r):
                return dve.tensor_tensor(w_lo[:, r, :], raw[:, r, :], w_hi[:, r, :].bitcast(F32), ALU.subtract)

            def run(st, evac=None, work=None, ends=False, peel=False):
                def turn(i, last):
                    slot = 0
                    for g, kts in enumerate(st.kts):
                        for k in range(0, kts, HK):
                            if k == kts - HK and evac:
                                for n in range(2):
                                    evac(i, g, n, (s_mm, st.half(i, slot) * 2 + (n + 1 + 2 * RING)))
                            if not (last and slot + RING >= st.halves):
                                dve.wait_ge(s_hi, st.half(i, slot + RING + 1))
                                rest(slot % RING).then_inc(s_lo, 1)
                            if work:
                                work(i, slot)
                            slot += 1
                if ends:
                    with turns_of(dve, st.turns - 1) as i:
                        turn(i, False)
                    turn(st.turns - 1, True)
                else:
                    if peel:
                        turn(0, False)
                    with turns_of(dve, st.turns, int(peel)) as i:
                        turn(i, False)

            def rsqrt(pr, unit, y, a, t, ss, scale):
                pr.link(dve, dve.tensor_scalar(a, ss, scale, EPS, ALU.mult, ALU.add), "rs", unit)
                pr.link(dve, dve.tensor_scalar(y.bitcast(I32), a.bitcast(I32), -0.5, RSQRT_SEED, ALU.mult, ALU.add),
                        "rs", unit)
                for _ in range(3):
                    pr.link(dve, dve.tensor_tensor(t, y, y, ALU.mult), "rs", unit)
                    pr.link(dve, dve.scalar_tensor_tensor(t, t, -0.5, a, ALU.mult, ALU.mult), "rs", unit)
                    pr.link(dve, dve.scalar_tensor_tensor(y, t, 1.5, y, ALU.add, ALU.mult), "rs", unit)

            def part(pr, act_pr, hi, lo, col, kt):
                dve.wait_ge(*act_pr.after(0, "hi", kt | 1))
                c = (kt % 8) * L
                pr.inc(dve.scalar_tensor_tensor(lo[:, kt, :], side_flat[:, c:c + L], prm_t[:, col + kt:col + kt + 1],
                                                hi[:, kt, :].bitcast(F32), ALU.mult, ALU.subtract), "lo")

            prm_dve.begin()
            dve.wait_ge(*prm_pe.after(0, "tr"))
            prm_dve.inc(dve.tensor_copy(prm_t[:, 0:PC_BM], side[:, 0, 0:PC_BM]), "copy")
            prm_dve.inc(dve.tensor_scalar(prm_t[:, PC_BM:PC_D], side[:, 0, PC_BM:PC_D], 0.5, None, ALU.mult), "copy")
            prm_dve.inc(dve.tensor_copy(prm_t[:, PC_D:P], side[:, 0, PC_D:P]), "copy")
            dve.wait_ge(*prm_dve.after(0, "copy"))
            norm_dve.begin()
            for r in range(RING):
                for kt in range(HK * r, HK * (r + 1)):
                    part(norm_dve, norm_act, m_hi, m_lo, PC_MG, kt)
                dve.wait_ge(s_hi, r + 1)
                rest(r).then_inc(s_lo, 1)

            def row_scales(i, slot):
                if i == 0 and slot == RT - 1:
                    dve.wait_ge(*norm_act.units(1))
                    rsqrt(norm_dve, 0, stat[:, 2:4], stat[:, 80:82], stat[:, 82:84], stat[:, 0:2], 1.0 / D)
                    norm_dve.end()
                elif slot == 5:
                    xn_dve.begin()
                    dve.wait_ge(*xn_act.units(i + 1))
                    rsqrt(xn_dve, i, stat[:, 6:7], stat[:, 80:81], stat[:, 82:83], stat[:, 4:5], 1.0 / D)
                    rows = x_flat[:, bass.ds(i * D, D)]
                    xn_dve.inc(dve.tensor_scalar(rows, rows, stat[:, 6:7], None, ALU.mult), "scale")
                    xn_dve.end()

            run(stage["km"], work=row_scales, peel=True)
            dve.wait_ge(*prm_pe.after(0, "line"))
            prm_dve.link(dve, dve.tensor_copy(gain_t[:, 0:6], side[:, 0, P:P + 6]), "gain", 0)
            prm_dve.inc(dve.tensor_tensor(gain_t[:, 6:7], gain_t[:, 0:1], gain_t[:, 1:2], ALU.mult), "gains")
            prm_dve.inc(dve.tensor_tensor(gain_t[:, 2:4], gain_t[:, 2:4], gain_t[:, 4:6], ALU.mult), "gains")
            prm_dve.inc(dve.tensor_copy(line, side[0:HEADS, 1, 0:LINE]), "line")
            prm_dve.end()

            def x_parts(i, slot):
                if i == 0:
                    if slot == 0:
                        xp_dve.begin()
                    for kt in (2 * slot, 2 * slot + 1):
                        part(xp_dve, xp_act, x_hi, x_lo, PC_G, kt)

            kp_dve.begin()
            dve.wait_ge(*kp_act.after(0, "ss"))
            rsqrt(kp_dve, 0, stat[:, 24:32], stat[:, 80:88], stat[:, 88:96], stat[:, 8:16], 1.0 / MHD)
            for r in range(RT):
                for h in range(4):
                    s = slice(h * MHD, (h + 1) * MHD)
                    kp_dve.inc(dve.tensor_scalar(kv_rows[:, r, s], kv_rows[:, r, s],
                                                 stat[:, 24 + 4 * r + h:25 + 4 * r + h], None, ALU.mult), "scale")
            run(stage["vm"], work=x_parts, peel=True)
            dve.wait_ge(*kp_pe.after(0, "tr"))
            for f in range(2):
                kp_dve.inc(dve.tensor_scalar(
                    km_t.rearrange("p (h f n) -> p h f n", f=2, n=L)[:, :, f, :],
                    side_flat.rearrange("p (h f n) -> p h f n", f=2, n=L)[:, :, f, :],
                    gain_t[:, 2 + f:3 + f], None, ALU.mult), "kmt")
            kp_dve.end()
            run(stage["u"])
            dve.wait_ge(*sp_pool.after(0, "den"))
            sp_dve.begin()
            sp_dve.inc(dve.reciprocal(spt("den"), spt("den")), "rden")
            run(stage["mqz"])

            def conv(i, slot):
                if slot == 12:
                    cv_dve.begin()
                    dve.wait_ge(s_evac[0], stage["conv"].pair(i, 2) * 2 + 4)
                    cv_dve.link(dve, dve.tensor_tensor(cv[:, 0, :], cv[:, 0, :], cv[:, 2, :], ALU.mult), "v", i)
                    for n in range(2):
                        v0, a0 = cv[:, 0, n * L:(n + 1) * L], cv[:, 2, n * L:(n + 1) * L]
                        for k in range(3):
                            w = prm_t[:, bass.ds(i * 2 + (PC_CONV + WT * (2 - k) + n), 1)]
                            if k == 0:
                                ins = dve.tensor_scalar(a0, v0, w, None, ALU.mult)
                            else:
                                ins = dve.scalar_tensor_tensor(a0[:, k:L], v0[:, 0:L - k], w, a0[:, k:L],
                                                               ALU.mult, ALU.add)
                            cv_dve.link(dve, ins, "acc", i)
                elif slot == 13:
                    cv_dve.link(dve, dve.tensor_tensor(cv[:, 2, :], cv[:, 2, :], cv[:, 1, :], ALU.mult), "y", i)
                elif slot == 15:
                    dve.wait_ge(*cv_act.after(i, "th"))
                    dve.wait_ge(s_evac[1], stage["conv"].pair(i, 3) * 2 + 4)
                    cv_dve.link(dve, dve.scalar_tensor_tensor(cv[:, 3, :], cv_th, 1.0, cv[:, 3, :], ALU.add, ALU.mult),
                                "sz", i)
                    cv_dve.inc(dve.tensor_tensor(cv[:, 2, :], cv[:, 2, :], cv[:, 3, :], ALU.mult), "yz")
                    dve.wait_ge(*cv_act.after(i, "hi"))
                    cv_dve.inc(dve.scalar_tensor_tensor(
                        ya_lo[:, bass.ds(i * 2, 2), :].rearrange("p t n -> p (t n)"), cv[:, 2, :], 0.5,
                        ya_hi[:, bass.ds(i * 2, 2), :].rearrange("p t n -> p (t n)").bitcast(F32),
                        ALU.mult, ALU.subtract), "lo")
                    cv_dve.end()

            def mem_attention(i, slot):
                if slot == 3:
                    ma_dve.begin()
                    dve.wait_ge(*ma_pe.after(i, "qk"))
                    rsqrt(ma_dve, i, stat[:, 32:34], stat[:, 80:82], stat[:, 82:84], side[:, 0, 0:2], 1.0 / MHD)
                    ma_dve.inc(dve.tensor_scalar(stat[:, 34:36], stat[:, 32:34], MHD ** -0.5, None, ALU.mult), "sc")
                    ma_dve.link(dve, dve.reduce_max(stat[:, 36:38], side[:, 1, :].rearrange("p (r n) -> p r n", r=RT),
                                                    AX.X), "mx", i)
                    ma_dve.inc(dve.scalar_tensor_tensor(stat[:, 38:40], stat[:, 36:38], -1.0, stat[:, 34:36],
                                                        ALU.mult, ALU.mult), "nb")
                elif slot == 7:
                    dve.wait_ge(*ma_act.after(i, "th"))
                    ma_dve.link(dve, dve.reciprocal(stat[:, 42:44], stat[:, 40:42]), "rsum", i)
                    for r in range(RT):
                        e = ma_e[:, r * L:(r + 1) * L]
                        ma_dve.inc(dve.tensor_scalar(e, e, stat[:, 42 + r:43 + r], None, ALU.mult), "p")
                    ma_dve.inc(dve.scalar_tensor_tensor(ma_sz, ma_sz, 1.0, mz[:, bass.ds(i * (2 * L), 2 * L)],
                                                        ALU.add, ALU.mult), "sz")
                elif slot == 13:
                    dve.wait_ge(*ma_pe.after(i, "pv"))
                    dve.wait_ge(*ma_dve.after(i, "sz"))
                    ma_dve.inc(dve.tensor_tensor(ma_sz, side[:, 3, :], ma_sz, ALU.mult), "y")
                elif slot == 14:
                    dve.wait_ge(*ma_act.after(i, "hi"))
                    ma_dve.inc(dve.scalar_tensor_tensor(
                        yb_lo[:, bass.ds(i * 2, 2), :].rearrange("p t n -> p (t n)"), ma_sz, 0.5,
                        yb_hi[:, bass.ds(i * 2, 2), :].rearrange("p t n -> p (t n)").bitcast(F32),
                        ALU.mult, ALU.subtract), "lo")
                    ma_dve.end()

            def conv_work(i, slot):
                mem_attention(i, slot)
                conv(i, slot)

            run(stage["conv"], work=conv_work)
            run(stage["aq"])
            run(stage["akv"])
            dve.wait_ge(*ak_act.after(0, "ss"))
            ak_dve.begin()
            rsqrt(ak_dve, 0, stat[:, 24:32], stat[:, 80:88], stat[:, 88:96], stat[:, 16:24], 1.0 / HD)
            for r in range(RT):
                for h in range(KVH):
                    ak_dve.inc(dve.tensor_scalar(
                        k_twice[:, r, h, :, :],
                        k_rows[:, r, h * HD:(h + 1) * HD].rearrange("p (a n) -> p a n", a=1).broadcast_to([P, 2, HD]),
                        stat[:, 24 + 4 * r + h:25 + 4 * r + h], None, ALU.mult), "scale")
            run(stage["az"])
            dve.wait_ge(*ak_pe.after(0, "tr"))
            ak_dve.inc(dve.tensor_scalar(k_dup, side_flat[:, 0:KVH * L], gain_t[:, 6:7], None, ALU.mult), "kt")
            ak_dve.end()
            dve.wait_ge(s_bias, 16)
            dve.memset(bias_t[0:CHUNK, :, 2 * CHUNK:WINDOW], NEG).then_inc(s_neg, 1)
            dve.memset(bias_t[CHUNK:P, :, 0:CHUNK], NEG).then_inc(s_neg, 1)
            dve.memset(sw_l[:, 0:2, 0:CHUNK], NEG).then_inc(s_neg, 1)
            dve.memset(sw_e[:, :, 0:CHUNK], 0.0).then_inc(s_neg, 1)
            dve.wait_ge(s_neg, 4)

            def merge_evac(first):
                def evac(i, g, n, done):
                    if g % 2 == 0:
                        return
                    st = stage[first]
                    v = val[:, n * L:(n + 1) * L]
                    m = merged[:, bass.ds(i * 1024 + (g // 2 * 2 + n) * L, L)]
                    dve.wait_ge(*done)
                    dve.wait_ge(s_evac[0], st.pair(i, g - 1) * 2 + (n + 3))
                    if first == "merge_conv":
                        dve.scalar_tensor_tensor(m, gate[:, n * L:(n + 1) * L], 1.0, acc[:, 2 + n, 0:GC],
                                                 ALU.add, ALU.mult).then_inc(s_evac[1], 1)
                        return
                    dve.scalar_tensor_tensor(v, gate[:, n * L:(n + 1) * L], 1.0, acc[:, 2 + n, 0:GC],
                                             ALU.add, ALU.mult).then_inc(s_evac[1], 1)
                    dve.wait_ge(s_evac[1], st.pair(i, g) * 2 + (n + 3))
                    dve.tensor_tensor(m, m, v, ALU.add).then_inc(s_sum, 1)
                return evac

            def window_head(i, t, s):
                sk = sink_all[:, bass.ds(t * 2, 2)].rearrange("p (a n) -> p a n", a=1).broadcast_to([P, 2, 2])
                four = lambda c: stat[:, c:c + 4].rearrange("p (a n) -> p a n", a=2)
                if s == 0:
                    sw_dve.begin()
                    dve.wait_ge(*sw_qk.after(t, "qk"))
                    rsqrt(sw_dve, t, four(44), four(80), four(84), side[:, 1:3, WINDOW:WINDOW + 2], 1.0 / HD)
                    sw_dve.link(dve, dve.tensor_scalar(stat[:, 48:52], stat[:, 44:48], HD ** -0.5, None, ALU.mult),
                                "sc", t)
                    for w in range(4):
                        lo = CHUNK if w < 2 else 0
                        c = (w // 2) * 256
                        sw_dve.inc(dve.scalar_tensor_tensor(
                            sw_l[:, w, lo:WINDOW], side[:, 1 + w % 2, c + lo:c + WINDOW], stat[:, 48 + w:49 + w],
                            bias_t[:, bass.ds(t * 2 + w % 2, 1), lo:WINDOW].rearrange("p a n -> p (a n)"),
                            ALU.mult, ALU.add), "l")
                elif s == 1:
                    dve.wait_ge(*sw_dve.after(t, "l"))
                    sw_dve.link(dve, dve.reduce_max(stat[:, 52:56], sw_l, AX.X), "mx", t)
                    sw_dve.link(dve, dve.tensor_tensor(four(56), four(52), sk, ALU.max), "mx", t)
                    sw_dve.inc(dve.tensor_scalar(stat[:, 60:64], stat[:, 56:60], -1.0, None, ALU.mult), "nb")
                    sw_dve.inc(dve.tensor_tensor(four(68), sk, four(56), ALU.subtract), "ds")
                elif s == 3:
                    dve.wait_ge(*sw_act.after(t, "es"))
                    sw_dve.link(dve, dve.tensor_tensor(stat[:, 64:68], stat[:, 64:68], stat[:, 72:76], ALU.add), "sum", t)
                    sw_dve.link(dve, dve.reciprocal(stat[:, 76:80], stat[:, 64:68]), "rsum", t)
                    rs = stat[:, 76:80].rearrange("p (w a) -> p w a", a=1).broadcast_to([P, 4, WINDOW])
                    sw_dve.inc(dve.tensor_tensor(sw_e[:, :, CHUNK:256], sw_e[:, :, CHUNK:256], rs, ALU.mult), "p")
                    sw_dve.end()

            def window_tail(t, s):
                if s == 1:
                    st_dve.begin()
                    dve.wait_ge(*st_act.after(t, "th"))
                    st_dve.inc(dve.scalar_tensor_tensor(sw_sz, sw_sz, 1.0, az[:, bass.ds(t * L, L)],
                                                        ALU.add, ALU.mult), "sz")
                elif s == 4:
                    dve.wait_ge(*st_pe.after(t, "pv"))
                    dve.wait_ge(*st_dve.after(t, "sz"))
                    st_dve.inc(dve.tensor_tensor(aq[:, bass.ds(t * L, L)], side[:, 3, 0:L], sw_sz, ALU.mult), "y")
                    st_dve.end()

            run(stage["merge_conv"], merge_evac("merge_conv"), work=window_slots(window_head, window_tail), peel=True)
            for s in range(6):
                window_tail(7, s)
            at_dve.begin()
            for h in range(2):
                dve.wait_ge(*at_act.after(0, "hi", h))
                at_dve.inc(dve.scalar_tensor_tensor(
                    ya_lo[:, 4 * h:4 * h + 4, :].rearrange("p t n -> p (t n)"), aq[:, h * 1024:(h + 1) * 1024], 0.5,
                    ya_hi[:, 4 * h:4 * h + 4, :].rearrange("p t n -> p (t n)").bitcast(F32),
                    ALU.mult, ALU.subtract), "lo")
            at_dve.end()

            per_state = lambda b: b.rearrange("p (s n) -> p s n", s=4)
            bu_re, bu_im = side[:, :, 0:L], side[:, :, L:2 * L]

            def state_space(first):
                def work(i, slot):
                    n = i + first
                    if slot == 0:
                        ss_dve.begin()
                        dve.wait_ge(*ss_pool.after(n, "ph"))
                        ss_dve.link(dve, dve.tensor_scalar(whole, phase, ROUND, -ROUND, ALU.add, ALU.add), "ph", n)
                        ss_dve.inc(dve.tensor_tensor(phase, phase, whole, ALU.subtract), "ph")
                    elif slot == 2:
                        dve.wait_ge(*ss_act.after(n, "sq"))
                        ss_dve.link(dve, dve.tensor_scalar(cosines, cosines, -2.0, 1.0, ALU.mult, ALU.add), "c", n)
                        dve.wait_ge(*ss_pe.after(n, "bu"))
                        ss_dve.inc(dve.tensor_tensor(per_state(in_re), per_state(cosines), bu_re, ALU.mult), "pre")
                        ss_dve.inc(dve.tensor_tensor(per_state(st_re), per_state(sines), bu_im, ALU.mult), "pre")
                    elif slot == 3:
                        ss_dve.inc(dve.tensor_tensor(per_state(in_im), per_state(cosines), bu_im, ALU.mult), "pre")
                        ss_dve.inc(dve.tensor_tensor(per_state(st_im), per_state(sines), bu_re, ALU.mult), "pre")
                    elif slot in (4, 5):
                        src, dst = (in_re, st_re) if slot == 4 else (in_im, st_im)
                        dve.wait_ge(*ss_pool.after(n, "z", slot - 4))
                        for s in range(4):
                            ss_dve.inc(dve.tensor_tensor_scan(
                                dst[:, s * L:(s + 1) * L],
                                ssm_t[:, bass.ds(n * 4 + s, 1)].broadcast_to([P, L]),
                                src[:, s * L:(s + 1) * L], 0.0, ALU.mult, ALU.add), "scan")
                    elif slot == 6:
                        dve.wait_ge(*ss_dve.after(n, "scan"))
                        ss_dve.inc(dve.tensor_tensor(b_channels, sines, st_re, ALU.mult), "szr")
                        ss_dve.link(dve, dve.tensor_tensor(whole, cosines, st_im, ALU.mult), "czi", n)
                        ss_dve.inc(dve.scalar_tensor_tensor(b_channels, b_channels, -1.0, whole,
                                                            ALU.mult, ALU.subtract), "xi")
                    elif slot == 10:
                        dve.wait_ge(*ss_pe.after(n, "y"))
                        un = u[:, bass.ds(n * L, L)]
                        ss_dve.inc(dve.scalar_tensor_tensor(un, un, prm_t[:, bass.ds(n + PC_D, 1)], side[:, 0, 0:L],
                                                            ALU.mult, ALU.add), "ys")
                        ss_dve.end()
                return work

            run(stage["merge_mem"], merge_evac("merge_mem"), work=state_space(0))
            run(stage["merge_att"], merge_evac("merge_att"), work=state_space(4))

            def sz_evac(i, g, n, done):
                if n == 0:
                    zz_dve.begin()
                dve.wait_ge(s_evac[g % 2], stage["sz"].pair(i, g) * 2 + (n + 3))
                dve.wait_ge(*zz_act.after(i * 2 + g, "th", n))
                z = sz_gate[:, bass.ds(i * 1024 + (2 * g + n) * L, L)]
                zz_dve.inc(dve.scalar_tensor_tensor(z, gate[:, n * L:(n + 1) * L], 1.0, z, ALU.add, ALU.mult), "sz")
                if n == 1:
                    zz_dve.end()

            def gelu(i, slot):
                ui = u[:, bass.ds(i * 1024, 1024)]
                if slot == 1:
                    ge_dve.begin()
                    dve.wait_ge(*ge_act.after(i, "sq"))
                    ge_dve.link(dve, dve.tensor_scalar(in_re, in_re, 0.044715, 1.0, ALU.mult, ALU.add), "a", i)
                    ge_dve.inc(dve.tensor_tensor(st_re, in_re, ui, ALU.mult), "a")
                elif slot == 4:
                    dve.wait_ge(*ge_act.after(i, "th"))
                    ge_dve.inc(dve.scalar_tensor_tensor(in_re, st_re, 1.0, ui, ALU.add, ALU.mult), "h")
                elif slot == 6:
                    dve.wait_ge(*ge_act.after(i, "hi"))
                    ge_dve.inc(dve.scalar_tensor_tensor(
                        yb_lo[:, bass.ds(i * 4, 4), :].rearrange("p t n -> p (t n)"), in_re, 0.5,
                        yb_hi[:, bass.ds(i * 4, 4), :].rearrange("p t n -> p (t n)").bitcast(F32),
                        ALU.mult, ALU.subtract), "lo")
                    ge_dve.end()

            run(stage["sz"], sz_evac, work=gelu)

            def glu_evac(i, g, n, done):
                if g == 0:
                    return
                if n == 0:
                    gl_dve.begin()
                    dve.wait_ge(*gl_act.units(i))
                dve.wait_ge(s_evac[1], stage["glu"].pair(i, 1) * 2 + (n + 3))
                dve.scalar_tensor_tensor(val[:, n * L:(n + 1) * L], gate[:, n * L:(n + 1) * L], 1.0,
                                         acc[:, n, 0:GC], ALU.add, ALU.mult).then_inc(s_evac[0], 1)

            def glu_work(i, slot):
                if slot == 3:
                    dve.wait_ge(s_evac[0], stage["glu"].pair(i, 0) * 2 + 4)
                    gl_dve.inc(dve.tensor_tensor(val, val, sz_gate[:, bass.ds(i * 512, 512)], ALU.mult), "w")
                    dve.wait_ge(*gl_act.after(i, "hi"))
                    gl_dve.inc(dve.scalar_tensor_tensor(
                        ya_lo[:, bass.ds(i * 2, 2), :].rearrange("p t n -> p (t n)"), val, 0.25,
                        ya_hi[:, bass.ds(i * 2, 2), :].rearrange("p t n -> p (t n)").bitcast(F32),
                        ALU.mult, ALU.subtract), "lo")
                    gl_dve.end()

            run(stage["glu"], glu_evac, work=glu_work)

            def merged_parts(i, slot):
                if slot in (8, 11):
                    h = slot // 11
                    if h == 0:
                        mg_dve.begin()
                    dve.wait_ge(*mg_act.after(i, "hi", h))
                    mg_dve.inc(dve.scalar_tensor_tensor(
                        m_lo[:, bass.ds(i * 4 + 2 * h, 2), :].rearrange("p t n -> p (t n)"),
                        merged[:, bass.ds(i * 1024 + 512 * h, 512)], 0.5,
                        m_hi[:, bass.ds(i * 4 + 2 * h, 2), :].rearrange("p t n -> p (t n)").bitcast(F32),
                        ALU.mult, ALU.subtract), "lo")

            run(stage["merge_ssm"], merge_evac("merge_ssm"), work=merged_parts)
            dve.wait_ge(s_xres, 16)

            def out_evac(i, g, n, done):
                dve.wait_ge(*done)
                o = x_rows[:, n, bass.ds(i * 512 + g * GC, GC)]
                dve.tensor_tensor(o, acc[:, 2 * (g % 2) + n, 0:GC], o, ALU.add).then_inc(s_evac[g % 2], 1)

            run(stage["out"], out_evac, ends=True)

        @block.gpsimd
        def _(pool):
            pool.sem_inc(ss_pool.sem, ss_pool.base)
            pool.dma_start(rb[:, :], rel_bias).then_inc(s_small, 16)
            pool.dma_start(onehot, const_onehot).then_inc(s_small, 16)
            for n, g in enumerate([attn_q_g, attn_k_g]):
                for h in range(2):
                    pool.dma_start(gain[n:n + 1, h * HD:(h + 1) * HD], g).then_inc(s_small, 16)
            for n, g in enumerate([mem_q_g, mem_k_g]):
                pool.dma_start(gain[2 + 2 * n:4 + 2 * n, :], g.rearrange("a (t p) -> (a t) p", p=P)).then_inc(s_small, 16)
            pool.dma_start(spt("lr"),
                          lam_re[0].rearrange("(t a) p -> t (a p)", a=2)).then_inc(s_lam, 16)
            pool.dma_start(spt("li"),
                          lam_im[0].rearrange("(t a) p -> t (a p)", a=2)).then_inc(s_lam, 16)
            pool.dma_start(spt("dt")[:, 0:2],
                          log_dt[0].rearrange("(t a) -> t a", a=2)).then_inc(s_lam, 16)
            pool.dma_start(sink_all[:, :], bass.AP(tensor=sinks.tensor, offset=0,
                                                   ap=[[0, P], [1, HEADS]])).then_inc(s_lam, 16)
            pool.wait_ge(*prm_dve.units(1))
            sp_pool.begin()
            link = lambda ins, name: sp_pool.link(pool, ins, name, 0)

            def exp(x_, k, p, t, name):
                ts, tt = pool.tensor_scalar, pool.tensor_tensor
                link(ts(x_, x_, -88.0, 89.0, ALU.max, ALU.min), name)
                link(ts(k, x_, 1.4426950408889634, ROUND, ALU.mult, ALU.add), name)
                link(ts(k, k, -ROUND, None, ALU.add), name)
                for c in (-0.693359375, 2.12194440e-4):
                    link(ts(t, k, c, None, ALU.mult), name)
                    link(tt(x_, x_, t, ALU.add), name)
                link(ts(p, x_, 1.0 / 5040, 1.0 / 720, ALU.mult, ALU.add), name)
                for c in (1.0 / 120, 1.0 / 24, 1.0 / 6, 0.5, 1.0):
                    link(tt(p, p, x_, ALU.mult), name)
                    link(ts(p, p, c, None, ALU.add), name)
                link(tt(p, p, x_, ALU.mult), name)
                link(ts(p, p, 1.0, None, ALU.add), name)
                link(ts(t.bitcast(I32), k, 127.0, 8388608.0, ALU.add, ALU.mult), name)
                link(tt(x_, p, t, ALU.mult), name)

            pool.wait_ge(s_lam, 4 * 16)
            dt = spt("dt")[:, 0:2]
            exp(dt, spt("k")[:, 0:2], spt("p")[:, 0:2], spt("t")[:, 0:2], "dt")
            for a in range(2):
                h = slice(a * STATES, (a + 1) * STATES)
                link(pool.tensor_scalar(spt("mag")[:, h], spt("lr")[:, h], dt[:, a:a + 1], None, ALU.mult), "mag")
            exp(spt("mag"), spt("k"), spt("p"), spt("t"), "mag")
            for a in range(2):
                h = slice(a * STATES, (a + 1) * STATES)
                link(pool.tensor_scalar(spt("frac")[:, h], spt("li")[:, h], dt[:, a:a + 1], None, ALU.mult), "frac")
            link(pool.tensor_scalar(spt("k"), spt("frac"), 1.0 / TWO_PI, ROUND, ALU.mult, ALU.add), "frac")
            link(pool.tensor_scalar(spt("k"), spt("k"), -ROUND, None, ALU.add), "frac")
            c1 = 6.28125
            c2 = float(np.float32(np.round((TWO_PI - c1) * 2 ** 22) / 2 ** 22))
            for c in (c1, c2, TWO_PI - c1 - c2):
                link(pool.tensor_scalar(spt("t"), spt("k"), -c, None, ALU.mult), "frac")
                link(pool.tensor_tensor(spt("frac"), spt("frac"), spt("t"), ALU.add), "frac")
            link(pool.tensor_scalar(spt("frac"), spt("frac"), 1.0 / TWO_PI, None, ALU.mult), "frac")
            tt = lambda o, a, b, op, name: link(pool.tensor_tensor(spt(o), spt(a), spt(b), op), name)
            tt("den", "lr", "lr", ALU.mult, "den")
            tt("t", "li", "li", ALU.mult, "den")
            tt("den", "den", "t", ALU.add, "den")
            pool.wait_ge(*sp_act.after(0, "sin"))
            tt("hs", "hs", "hs", ALU.mult, "ab")
            link(pool.tensor_scalar(spt("hs"), spt("hs"), -2.0, 1.0, ALU.mult, ALU.add), "ab")
            tt("p", "mag", "hs", ALU.mult, "ab")
            tt("sn", "mag", "sn", ALU.mult, "ab")
            link(pool.tensor_scalar(spt("p"), spt("p"), -1.0, None, ALU.add), "ab")
            pool.wait_ge(*sp_dve.after(0, "rden"))
            tt("t", "p", "lr", ALU.mult, "f")
            tt("k", "sn", "li", ALU.mult, "f")
            tt("t", "t", "k", ALU.add, "f")
            tt("fr", "t", "den", ALU.mult, "f")
            tt("t", "sn", "lr", ALU.mult, "f")
            tt("k", "p", "li", ALU.mult, "f")
            tt("t", "t", "k", ALU.subtract, "f")
            tt("fi", "t", "den", ALU.mult, "f")
            sp_pool.end()

            pool.wait_ge(s_evac[1], 2 * (stage["conv"].group0 // 2) + 2)
            pool.wait_ge(s_evac[0], 2 * (stage["conv"].group0 // 2) + 2)
            with pool.Fori(0, 4) as i:
                ma_pool.begin()
                gate_on(pool, *ma_pe.units(i))
                qi = mq[:, bass.ds(i * (2 * L), 2 * L)]
                ma_pool.inc(pool.tensor_copy(ma_q, qi), "q")
                ma_pool.inc(pool.tensor_tensor(ma_sq, qi, qi, ALU.mult), "sq")
                ma_pool.inc(pool.tensor_copy(ma_v.rearrange("p (r n) -> p r n", r=RT),
                                             kv_rows[:, :, bass.ds(i * MHD + W, MHD)]), "v")
                ma_pool.end()

            pool.wait_ge(s_bc, 6 * 16)
            pool.wait_ge(*sp_act.after(0, "copy"))
            bb_pool.begin()
            f_of = lambda c: ssm_t[:, 32 * c:32 * (c + 1)].rearrange("p (t a) -> p t a", a=1).broadcast_to([P, 32, GH])
            as3 = lambda b: b.rearrange("p (t h) -> p t h", h=GH)
            bg, bv = as3(gate), as3(val)
            pool.wait_ge(s_line, 16)
            bb_pool.inc(pool.tensor_tensor(bg, ssm_b[:, 1], f_of(3), ALU.mult), "prod")
            bb_pool.inc(pool.tensor_tensor(bv, ssm_b[:, 0], f_of(3), ALU.mult), "prod")
            pool.wait_ge(*bb_pool.after(0, "prod", 1))
            bb_pool.inc(pool.tensor_tensor(ssm_b[:, 0], ssm_b[:, 0], f_of(2), ALU.mult), "prod")
            bb_pool.inc(pool.tensor_tensor(ssm_b[:, 1], ssm_b[:, 1], f_of(2), ALU.mult), "prod")
            pool.wait_ge(*bb_pool.after(0, "prod"))
            bb_pool.inc(pool.tensor_tensor(ssm_b[:, 0], ssm_b[:, 0], bg, ALU.subtract), "sum")
            bb_pool.inc(pool.tensor_tensor(ssm_b[:, 1], ssm_b[:, 1], bv, ALU.add), "sum")
            pool.wait_ge(*bb_pool.after(0, "sum"))
            pool.wait_ge(s_evac[0], 2 * (stage["akv"].group0 // 2) + 2)
            pool.wait_ge(s_evac[1], 2 * (stage["az"].group0 // 2) + 2)
            with pool.Fori(0, 4) as i:
                for sub in range(2):
                    t = i * 2 + sub
                    sw_pool.begin()
                    gate_on(pool, *sw_qk.units(t))
                    sw_pool.inc(pool.tensor_copy(sw_q, aq[:, bass.ds(t * L, L)]), "q")
                    q = aq[:, bass.ds(t * L, L)]
                    sw_pool.inc(pool.tensor_tensor(sw_sq, q, q, ALU.mult), "sq")
                    gate_on(pool, *ak_dve.units(1))
                    sw_pool.inc(pool.tensor_copy(sw_k, k_dup[:, bass.ds(i * L, L)]), "k")
                    gate_on(pool, *st_pe.units(t))
                    sw_pool.inc(pool.tensor_copy(sw_v[:, :, :], v_rows[:, :, bass.ds(i * HD, HD)]), "v")
                    sw_pool.end()

            pool.wait_ge(*st_dve.after(7, "sz"))
            with pool.Fori(0, 8) as n:
                ss_pool.begin()
                for c in range(2):
                    bt = ssm_b[:, c, bass.ds(n * 4, 4), :].rearrange("p (s a) h -> p s a h", a=1)
                    ss_pool.inc(pool.tensor_tensor(
                        masked_b[:, c * 512:(c + 1) * 512].rearrange("p (s j h) -> p s j h", s=4, j=8),
                        bt.broadcast_to([P, 4, 8, GH]),
                        state_group.rearrange("p s (j a) -> p s j a", a=1).broadcast_to([P, 4, 8, GH]), ALU.mult), "mask")
                for c in range(2):
                    ct = ssm_c[:, c, bass.ds(n, 1), :]
                    ss_pool.inc(pool.tensor_tensor(
                        masked_c[:, c * 512:(c + 1) * 512].rearrange("p (j n) -> p j n", j=8),
                        ct.broadcast_to([P, 8, STATES]),
                        channel_group.rearrange("p (j a) -> p j a", a=1).broadcast_to([P, 8, STATES]), ALU.mult), "mask")
                def link(ins, name):
                    ss_pool.inc(ins, name)
                    gate_on(pool, ss_pool.sem, n * ss_pool.per + (ss_pool.base + ss_pool.k))

                gate_on(pool, *at_dve.units(1))
                th = ssm_t[:, bass.ds(n * 4 + 32, 4)].rearrange("p (s a) -> p s a", a=1).broadcast_to([P, 4, L])
                tm = time.rearrange("p (a n) -> p a n", a=1).broadcast_to([P, 4, L])
                ss_pool.inc(pool.tensor_tensor(phase.rearrange("p (s n) -> p s n", s=4), th, tm, ALU.mult), "ph")
                gate_on(pool, *ss_dve.after(n, "pre", 1))
                ss_pool.inc(pool.tensor_tensor(in_re, in_re, st_re, ALU.add), "z")
                gate_on(pool, *ss_dve.after(n, "pre"))
                ss_pool.inc(pool.tensor_tensor(in_im, in_im, st_im, ALU.subtract), "z")
                gate_on(pool, *ss_dve.after(n, "scan", 3))
                ss_pool.inc(pool.tensor_tensor(in_re, cosines, st_re, ALU.mult), "x")
                gate_on(pool, *ss_dve.after(n, "scan"))
                link(pool.tensor_tensor(in_im, sines, st_im, ALU.mult), "x")
                ss_pool.inc(pool.tensor_tensor(in_re, in_re, in_im, ALU.subtract), "x")
                ss_pool.end()


_INS = ['x', 'mem', 'norm_g', 'mem_norm_g', 'w_in', 'lam_re', 'lam_im', 'log_dt', 'b_re', 'b_im', 'c_re', 'c_im',
        'd_skip', 'w_glu', 'conv_w', 'attn_q_g', 'attn_k_g', 'sinks', 'rel_bias', 'w_mem_kv', 'mem_q_g', 'mem_k_g',
        'w_branch', 'w_merge', 'b_merge', 'w_out']


def kernel(**inputs):
    import concourse.bacc as bacc
    from concourse.bass_utils import run_bass_kernel_spmd

    nc = bacc.Bacc("TRN2", target_bir_lowering=False, num_devices=1)
    arrays, args = {}, []
    given = [(n, np.ascontiguousarray(inputs[n])) for n in _INS]
    given += list(zip(["const_block", "const_onehot"], constants()))
    for name, a in given:
        arrays[f"in_{name}"] = a
        args.append(nc.dram_tensor(f"in_{name}", a.shape, mybir.dt.from_np(a.dtype), kind="ExternalInput").ap())
    args.append(nc.dram_tensor("out_0", (1, L, D), F32, kind="ExternalOutput").ap())
    hybrid_block(nc, *args)
    r = run_bass_kernel_spmd(nc, [arrays], core_ids=[0])
    return r.results[0]["out_0"]
```
